# Optimizing a Trainium2 kernel written in Bass

```python
import math
import jax, jax.numpy as jnp
from jax import lax
import numpy as np

D_MODEL = 2048
BATCH = 1
SEQ = 256
DEPTH = 1

N_META = 16
BLOCK_Q = 128
ROPE_THETA = 500000.0
EPS = 1e-6
N_DIFF_HEADS = 8
DIFF_HEAD_DIM = 64
DIFF_V_DIM = 2 * DIFF_HEAD_DIM
DIFF_ROT_DIM = DIFF_HEAD_DIM // 4
N_FOX_HEADS = 8
FOX_HEAD_DIM = 128
N_BRANCH = 2
DIFF_QK_W = N_DIFF_HEADS * 2 * DIFF_HEAD_DIM
DIFF_V_W = N_DIFF_HEADS * DIFF_V_DIM
FOX_W = N_FOX_HEADS * FOX_HEAD_DIM
W_IN_SPLITS = (DIFF_QK_W, DIFF_QK_W, DIFF_V_W, FOX_W, FOX_W, FOX_W, N_FOX_HEADS, D_MODEL, D_MODEL)
W_IN_COLS = sum(W_IN_SPLITS)
PEER_HEADS = 8
PEER_N_KEYS = 128
PEER_N_EXPERTS = PEER_N_KEYS * PEER_N_KEYS
PEER_KEY_DIM = 128
PEER_HALF = PEER_KEY_DIM // 2
PEER_TOPK = 16
PEER_CHUNK = 128

kernel_name = 'hybrid_diff_fox_peer_meta'

def rms_norm(x, g):
    x32 = x.astype(jnp.float32)
    y = x32 * lax.rsqrt(jnp.mean(x32 * x32, axis=-1, keepdims=True) + EPS)
    return (y * g.astype(jnp.float32)).astype(x.dtype)

def rope_tables(length, rot_dim):
    inv = ROPE_THETA ** (-jnp.arange(0, rot_dim, 2, dtype=jnp.float32) / rot_dim)
    ang = jnp.arange(length, dtype=jnp.float32)[:, None] * inv[None, :]
    return jnp.cos(ang), jnp.sin(ang)

def partial_rope(x, cos, sin):
    half = cos.shape[-1]
    r = 2 * half
    shape = (1, cos.shape[0]) + (1,) * (x.ndim - 3) + (half,)
    c, s = cos.reshape(shape), sin.reshape(shape)
    xr = x[..., :r].astype(jnp.float32)
    x1, x2 = xr[..., :half], xr[..., half:]
    rot = jnp.concatenate([x1 * c - x2 * s, x2 * c + x1 * s], axis=-1).astype(x.dtype)
    return jnp.concatenate([rot, x[..., r:]], axis=-1)

def block_ranges(length):
    n_blocks = (length - N_META) // BLOCK_Q
    return [(0, N_META)] + [(N_META + i * BLOCK_Q, N_META + (i + 1) * BLOCK_Q) for i in range(n_blocks)]

def causal_mask(lo, hi):
    qpos = jnp.arange(lo, hi)
    kpos = jnp.arange(hi)
    return kpos[None, :] <= qpos[:, None]

def diff_attention(q1, q2, k1, k2, v, lam):
    scale = DIFF_HEAD_DIM ** -0.5
    outs = []
    for lo, hi in block_ranges(q1.shape[1]):
        mask = causal_mask(lo, hi)

        def probs(q, k):
            s = jnp.einsum('bqhd,bkhd->bhqk', q[:, lo:hi], k[:, :hi]).astype(jnp.float32) * scale
            return jax.nn.softmax(jnp.where(mask, s, -jnp.inf), axis=-1)

        p = probs(q1, k1) - lam * probs(q2, k2)
        outs.append(jnp.einsum('bhqk,bkhd->bqhd', p.astype(v.dtype), v[:, :hi]))
    return jnp.concatenate(outs, axis=1)

def forgetting_attention(q, k, v, cum_logf):
    scale = FOX_HEAD_DIM ** -0.5
    outs = []
    for lo, hi in block_ranges(q.shape[1]):
        mask = causal_mask(lo, hi)
        s = jnp.einsum('bqhd,bkhd->bhqk', q[:, lo:hi], k[:, :hi]).astype(jnp.float32) * scale
        s = s + cum_logf[:, :, lo:hi, None] - cum_logf[:, :, None, :hi]
        p = jax.nn.softmax(jnp.where(mask, s, -jnp.inf), axis=-1)
        outs.append(jnp.einsum('bhqk,bkhd->bqhd', p.astype(v.dtype), v[:, :hi]))
    return jnp.concatenate(outs, axis=1)

def split_cols(y, sizes):
    points, acc = [], 0
    for sz in sizes[:-1]:
        acc += sz
        points.append(acc)
    return jnp.split(y, points, axis=-1)

def peer(h, w_query, sub_keys, expert_u, expert_v):
    b, length, d = h.shape
    t = h.reshape(b * length, d)
    n_tok = t.shape[0]
    q = (t @ w_query).reshape(n_tok, PEER_HEADS, 2, PEER_HALF)
    s = jnp.einsum('thcd,hcnd->thcn', q, sub_keys).astype(jnp.float32)
    v1, i1 = lax.top_k(s[:, :, 0], PEER_TOPK)
    v2, i2 = lax.top_k(s[:, :, 1], PEER_TOPK)
    cand = (v1[..., :, None] + v2[..., None, :]).reshape(n_tok, PEER_HEADS, PEER_TOPK * PEER_TOPK)
    best, j = lax.top_k(cand, PEER_TOPK)
    e_idx = (jnp.take_along_axis(i1, j // PEER_TOPK, axis=-1) * PEER_N_KEYS
             + jnp.take_along_axis(i2, j % PEER_TOPK, axis=-1))
    gate = jax.nn.softmax(best, axis=-1)
    pad = (-n_tok) % PEER_CHUNK
    tp = jnp.pad(t, ((0, pad), (0, 0))).reshape(-1, PEER_CHUNK, d)
    ep = jnp.pad(e_idx, ((0, pad), (0, 0), (0, 0))).reshape(-1, PEER_CHUNK, PEER_HEADS, PEER_TOPK)
    gp = jnp.pad(gate, ((0, pad), (0, 0), (0, 0))).reshape(-1, PEER_CHUNK, PEER_HEADS, PEER_TOPK)

    def chunk(args):
        tc, ec, gc = args
        u_sel = expert_u[ec]
        a = jax.nn.gelu(jnp.einsum('cd,chkd->chk', tc, u_sel).astype(jnp.float32), approximate=False)
        w = (gc * a).astype(tc.dtype)
        return jnp.einsum('chk,chkd->cd', w, expert_v[ec])

    out = lax.map(chunk, (tp, ep, gp))
    return out.reshape(-1, d)[:n_tok].reshape(b, length, d)

def setup_inputs(seed: int = 0) -> dict:
    key = jax.random.key(seed)
    ks = jax.random.split(key, 24)
    f32 = jnp.float32
    nrm = lambda k, shape, sc: jax.random.normal(k, shape, f32) * sc
    L_ = DEPTH
    return {
        'x': nrm(ks[0], (BATCH, SEQ, D_MODEL), 1.0),
        'meta_tokens': nrm(ks[1], (N_META, D_MODEL), 1.0),
        'norm_mix_g': 1.0 + nrm(ks[2], (L_, D_MODEL), 0.02),
        'w_in': nrm(ks[3], (L_, D_MODEL, W_IN_COLS), D_MODEL ** -0.5),
        'b_forget': 2.0 + nrm(ks[4], (L_, N_FOX_HEADS), 0.5),
        'b_gate': nrm(ks[5], (L_, N_BRANCH, D_MODEL), 0.02),
        'diff_q_norm_g': 1.0 + nrm(ks[6], (L_, DIFF_HEAD_DIM), 0.02),
        'diff_k_norm_g': 1.0 + nrm(ks[7], (L_, DIFF_HEAD_DIM), 0.02),
        'fox_q_norm_g': 1.0 + nrm(ks[8], (L_, FOX_HEAD_DIM), 0.02),
        'fox_k_norm_g': 1.0 + nrm(ks[9], (L_, FOX_HEAD_DIM), 0.02),
        'lambda_q1': nrm(ks[10], (L_, DIFF_HEAD_DIM), 0.1),
        'lambda_k1': nrm(ks[11], (L_, DIFF_HEAD_DIM), 0.1),
        'lambda_q2': nrm(ks[12], (L_, DIFF_HEAD_DIM), 0.1),
        'lambda_k2': nrm(ks[13], (L_, DIFF_HEAD_DIM), 0.1),
        'diff_subln_g': 1.0 + nrm(ks[14], (L_, DIFF_V_DIM), 0.02),
        'w_branch_diff': nrm(ks[15], (L_, DIFF_V_W, D_MODEL), DIFF_V_W ** -0.5),
        'w_branch_fox': nrm(ks[16], (L_, FOX_W, D_MODEL), FOX_W ** -0.5),
        'w_out': nrm(ks[17], (L_, D_MODEL, D_MODEL), D_MODEL ** -0.5),
        'norm_peer_g': 1.0 + nrm(ks[18], (L_, D_MODEL), 0.02),
        'peer_w_query': nrm(ks[19], (L_, D_MODEL, PEER_HEADS * PEER_KEY_DIM), D_MODEL ** -0.5),
        'peer_sub_keys': nrm(ks[20], (L_, PEER_HEADS, 2, PEER_N_KEYS, PEER_HALF), PEER_HALF ** -0.5),
        'peer_expert_u': nrm(ks[21], (L_, PEER_N_EXPERTS, D_MODEL), D_MODEL ** -0.5),
        'peer_expert_v': nrm(ks[22], (L_, PEER_N_EXPERTS, D_MODEL), PEER_HEADS ** -0.5),
    }

def reference(x, meta_tokens, norm_mix_g, w_in, b_forget, b_gate, diff_q_norm_g, diff_k_norm_g,
              fox_q_norm_g, fox_k_norm_g, lambda_q1, lambda_k1, lambda_q2, lambda_k2, diff_subln_g,
              w_branch_diff, w_branch_fox, w_out, norm_peer_g, peer_w_query, peer_sub_keys,
              peer_expert_u, peer_expert_v):
    b = x.shape[0]
    meta = jnp.broadcast_to(meta_tokens.astype(x.dtype)[None], (b, N_META, D_MODEL))
    h_res = jnp.concatenate([meta, x], axis=1)
    length = h_res.shape[1]
    cos, sin = rope_tables(length, DIFF_ROT_DIM)
    for l in range(DEPTH):
        h = rms_norm(h_res, norm_mix_g[l])
        dq, dk, dv, fq, fk, fv, f_logit, g_a, g_b = split_cols(h @ w_in[l], W_IN_SPLITS)
        dq = partial_rope(rms_norm(dq.reshape(b, length, N_DIFF_HEADS, 2, DIFF_HEAD_DIM), diff_q_norm_g[l]), cos, sin)
        dk = partial_rope(rms_norm(dk.reshape(b, length, N_DIFF_HEADS, 2, DIFF_HEAD_DIM), diff_k_norm_g[l]), cos, sin)
        dv = dv.reshape(b, length, N_DIFF_HEADS, DIFF_V_DIM)
        lam_init = 0.8 - 0.6 * math.exp(-0.3 * l)
        lam = (jnp.exp(jnp.sum(lambda_q1[l].astype(jnp.float32) * lambda_k1[l].astype(jnp.float32)))
               - jnp.exp(jnp.sum(lambda_q2[l].astype(jnp.float32) * lambda_k2[l].astype(jnp.float32)))
               + lam_init)
        o_diff = diff_attention(dq[..., 0, :], dq[..., 1, :], dk[..., 0, :], dk[..., 1, :], dv, lam)
        o_diff = rms_norm(o_diff, diff_subln_g[l]) * (1.0 - lam_init)
        y_diff = o_diff.reshape(b, length, DIFF_V_W) @ w_branch_diff[l]
        fq = rms_norm(fq.reshape(b, length, N_FOX_HEADS, FOX_HEAD_DIM), fox_q_norm_g[l])
        fk = rms_norm(fk.reshape(b, length, N_FOX_HEADS, FOX_HEAD_DIM), fox_k_norm_g[l])
        fv = fv.reshape(b, length, N_FOX_HEADS, FOX_HEAD_DIM)
        log_f = jax.nn.log_sigmoid((f_logit + b_forget[l]).astype(jnp.float32))
        cum_logf = jnp.transpose(jnp.cumsum(log_f, axis=1), (0, 2, 1))
        o_fox = forgetting_attention(fq, fk, fv, cum_logf)
        y_fox = o_fox.reshape(b, length, FOX_W) @ w_branch_fox[l]
        merged = jax.nn.sigmoid(g_a + b_gate[l, 0]) * y_diff + jax.nn.sigmoid(g_b + b_gate[l, 1]) * y_fox
        h_res = h_res + merged @ w_out[l]
        h2 = rms_norm(h_res, norm_peer_g[l])
        h_res = h_res + peer(h2, peer_w_query[l], peer_sub_keys[l], peer_expert_u[l], peer_expert_v[l])
    return h_res[:, N_META:]


_drawn_inputs = setup_inputs


def setup_inputs(seed=0):
    import zlib

    import numpy as np

    out = dict(_drawn_inputs(seed))
    spreads = {}
    factors = {'b_gate': 5.61,
     'diff_q_norm_g': 3.004,
     'diff_k_norm_g': 3.153,
     'fox_q_norm_g': 17.527,
     'fox_k_norm_g': 18.597,
     'lambda_q1': 6.328,
     'diff_subln_g': 9.302,
     'norm_peer_g': 11.389}
    for name, (base, spread) in spreads.items():
        noise = np.random.default_rng([zlib.crc32(name.encode()), seed]).standard_normal(out[name].shape)
        drawn = base * np.exp(spread * noise) if base else spread * noise
        out[name] = __import__('jax').numpy.asarray(drawn.astype(out[name].dtype))
    for name, factor in factors.items():
        out[name] = (out[name] * factor).astype(out[name].dtype)
    return out
```

```python
import numpy as np
from contextlib import ExitStack

import concourse.bass as bass
from concourse import mybir

F32 = mybir.dt.float32
F32R = mybir.dt.float32r
U32 = mybir.dt.uint32
BF16 = mybir.dt.bfloat16
ACT = mybir.ActivationFunctionType
ALU = mybir.AluOpType
AX = mybir.AxisListType
ds = bass.ds

P = 128
D = 2048
KC = D // P
META = 16
T = 256
L = META + T
HEADS = 8
PER_HEAD = 10
NK = 128
TOPK = 16
NSEL = HEADS * TOPK
EPS = 1e-6
LAM_INIT = 0.2
HALF = 1024
NEG = -1e30
LOWEST = -3.0e38

B_W_IN = HEADS * PER_HEAD
B_BRANCH, B_OUT, B_QUERY, B_U, B_V = KC, KC, HEADS, NK, NK
F_BRANCH = B_W_IN
F_OUT = F_BRANCH + B_BRANCH
F_QUERY = F_OUT + B_OUT
F_U = F_QUERY + B_QUERY
F_V = F_U + B_U
BLOCKS = F_V + B_V
F_G = F_U + B_U // 2

QK_AT = {"dq": (0, T), "dk": (T, L), "fq": (T + L, T), "fk": (2 * T + L, L)}
QK_W = 2 * (T + L)
KEYS = (META + P, META + 2 * P)
SC_W = sum(KEYS)

CONSTS = [("rope_cos", T + L), ("rope_sin", T + L), ("mask", SC_W), ("mean64", P), ("mean128", P), ("mean2048", P),
          ("swap", P), ("ident", P), ("iota", P), ("iota16", TOPK), ("eps", 1), ("one", L)]
PARAMS = [("g_mix", KC), ("g_peer", KC), ("b_gate", 2 * KC), ("g_dq", 1), ("g_dk", 1), ("g_fq", 1), ("g_fk", 1),
          ("g_sub", 1), ("b_forget", 1), ("lambdas", 256), ("w_forget", KC * HEADS), ("sub_keys", HEADS * NK)]


def columns(table):
    at, out = 0, {}
    for name, w in table:
        out[name] = (at, w)
        at += w
    return out, at


def shape_constants():
    at, width = columns(CONSTS)
    c = np.zeros((P, width), np.float32)

    def put(name, v):
        a, w = at[name]
        c[:, a:a + w] = v

    rot = 16
    inv = (np.float32(500000.0) ** (-np.arange(0, rot, 2, dtype=np.float32) / np.float32(rot))).astype(np.float32)
    ang = (np.arange(L, dtype=np.float32)[:, None] * inv[None, :]).astype(np.float32)
    cos, sin = np.cos(ang).T, np.sin(ang).T
    cc, ss = np.ones((P, L), np.float32), np.zeros((P, L), np.float32)
    swap = np.zeros((P, P), np.float32)
    for b in (0, 64):
        cc[b:b + 8], cc[b + 8:b + 16] = cos, cos
        ss[b:b + 8], ss[b + 8:b + 16] = -sin, sin
        for j in range(8):
            swap[b + j + 8, b + j] = 1.0
            swap[b + j, b + j + 8] = 1.0
    put("rope_cos", np.concatenate([cc[:, META:], cc], 1))
    put("rope_sin", np.concatenate([ss[:, META:], ss], 1))
    q, k = np.arange(P)[:, None], np.arange(L)[None, :]
    put("mask", np.concatenate([np.where(k[:, :n] <= q + META + b * P, 0.0, NEG) for b, n in enumerate(KEYS)], 1))
    bd = np.zeros((P, P), np.float32)
    bd[:64, :64] = bd[64:, 64:] = 1.0 / 64
    put("mean64", bd)
    put("mean128", 1.0 / 128)
    put("mean2048", 1.0 / 2048)
    put("swap", swap)
    put("ident", np.eye(P))
    put("iota", np.arange(P)[None, :])
    put("iota16", np.arange(TOPK)[None, :])
    put("eps", EPS)
    put("one", 1.0)
    return c


def spread(ap, dim, n):
    shape = list(ap.shape)
    shape[dim] = n
    return ap.broadcast_to(shape)


class Chain:

    def __init__(self, eng, sem):
        self.eng, self.sem, self.base, self.n = eng, sem, 0, 0

    def link(self, ins, before_max=False):
        self.n += 1
        ins.then_inc(self.sem, 1)
        self.eng.wait_ge(self.sem, self.base + self.n)
        if before_max:
            self.stand(self.n)

    def stand(self, n):
        self.eng.memset(self.spare[:, n:n + 1], 0.0)

    def enter(self, i, per_turn):
        self.start = self.base + self.n
        self.base, self.n, self.per_turn = self.start + i * per_turn, 0, per_turn

    def leave(self, turns):
        assert self.n == self.per_turn, (self.n, self.per_turn)
        self.base, self.n = self.start + turns * self.per_turn, 0


def hybrid_layer(nc, stream, x_t, params, consts, h1_rows, out):
    with ExitStack() as ctx:
        def sb(name, cols, dt=F32):
            return ctx.enter_context(nc.sbuf_tensor(name, [P, cols], dt))

        def sem(name):
            return ctx.enter_context(nc.semaphore(name))

        arena = sb("arena", NK * T)
        xr = sb("xr", 2 * KC * L, F32R)
        raw = sb("raw", 4 * HALF)
        whi = sb("whi", 4 * HALF, F32R)
        wlo = sb("wlo", 2 * HALF, F32R)
        small = sb("small", 1472)
        psum = ctx.enter_context(nc.psum_tensor("psum", [P, 8 * 512], F32))

        def bank(b, a=0, w=512):
            return psum[:, b * 512 + a:b * 512 + a + w]

        class Region:

            def __init__(self, a, b):
                self.a, self.b, self.first = a, b, a

            def take(self, w):
                a = self.a
                self.a += w
                assert self.a <= self.b, (self.a, self.b)
                return arena[:, a:a + w]

            def again(self):
                return Region(self.first, self.b)

            def sub(self, w):
                a = self.a
                self.take(w)
                return Region(a, a + w)

        MID = NK * T // 2
        low, high = Region(0, MID), Region(MID, NK * T)
        c_at, c_w = columns(CONSTS)
        p_at, p_w = columns(PARAMS)
        xT = low.take(KC * L).rearrange("p (k t) -> p k t", k=KC)
        r_gates = low.sub(2 * KC * T)
        p_sb = low.take(p_w)
        scal = low.take(16)
        r_low = low.sub(MID - low.a)
        r_work = high.sub(NK * T - MID - c_w - 2 * HEADS * T)
        r_o = high.sub(2 * HEADS * T)
        c_sb = high.take(c_w)
        C = {n: c_sb[:, a:a + w] for n, (a, w) in c_at.items()}
        C.update({n: p_sb[:, a:a + w] for n, (a, w) in p_at.items()})
        wf = C["w_forget"].rearrange("p (k h) -> p k h", k=KC)
        neg_lam = scal[:, 0:1]
        gates = r_gates.again().take(2 * KC * T).rearrange("p (g t) -> p g t", g=2 * KC)
        oT = r_o.again().take(2 * HEADS * T).rearrange("p (h j t) -> p h j t", h=HEADS, j=2)

        w0 = r_work.again()
        hn = w0.take(KC * L).rearrange("p (k t) -> p k t", k=KC)
        rstd0 = w0.take(L)
        fg = [w0.take(L) for _ in range(4)]
        lam_t = w0.take(64)
        w1 = r_work.again()
        qk_raw = w1.take(QK_W)
        qk_sq = w1.take(QK_W)
        qk_std = w1.take(QK_W)
        qk = w1.take(QK_W)
        assert w1.a <= r_work.a + KC * L
        w1.a = w0.a
        rope_a, rope_b = w1.take(T + L), qk_sq[:, 0:T + L]
        v = [w1.take(384) for _ in range(2)]
        cum_rows = r_low.again().take(HEADS * L)
        cum_q, cum_k = small[:, 0:T], w1.take(L)
        vT = [w1.take(L), small[:, T:T + L]]
        prob = [w1.take(SC_W) for _ in range(2)] + [small[:, 2 * T + L:2 * T + L + SC_W]]
        pT = [w1.take(640) for _ in range(2)]
        sm = w1.take(24)
        neg_max, zsum, zinv = sm[:, 0:6], sm[:, 6:12], sm[:, 12:18]
        w2 = r_work.again()
        merged = w2.take(KC * T).rearrange("p (k t) -> p k t", k=KC)
        h1T = w2.take(KC * T).rearrange("p (k t) -> p k t", k=KC)
        o_sq = r_low.again().take(HEADS * T)
        o_std = r_work.again().take(HEADS * T)
        br = [w2.take(T) for _ in range(2)]
        h2 = merged
        rows = r_work.again().take(2 * D)
        w3 = r_gates.again()
        h2_sq = w3.take(KC * T).rearrange("p (k t) -> p k t", k=KC)
        rstd2 = w3.take(T)
        qT = w3.take(HEADS * T).rearrange("p (h t) -> p h t", h=HEADS)
        st = r_o.again().take(4 * HEADS * NK).rearrange("p (i c n) -> p i c n", i=2 * HEADS, c=2)
        SPARE = 2 * KC * T
        w4 = Region(r_work.a + SPARE, r_work.b)
        chosen_i = w4.take(2 * 2 * NSEL).rearrange("p (c s) -> p c s", c=2)
        chosen_g = w4.take(2 * NSEL)
        gate_sum = w4.take(4 * HEADS)
        vals = w4.take(2 * TOPK).rearrange("p (c m) -> p c m", c=2)
        idxf = w4.take(2 * TOPK).rearrange("p (c m) -> p c m", c=2)
        idxu = w4.take(2 * TOPK).bitcast(U32).rearrange("p (c m) -> p c m", c=2)
        best = w4.take(TOPK)
        ju = w4.take(TOPK).bitcast(U32)
        jh = w4.take(2 * TOPK).bitcast(U32).rearrange("p (c m) -> p c m", c=2)
        jf = w4.take(2 * TOPK).rearrange("p (c m) -> p c m", c=2)
        sc = small[:, 0:2 * NK].rearrange("p (c n) -> p c n", c=2)
        sc_left = small[:, 256:256 + 2 * NK].rearrange("p (c n) -> p c n", c=2)
        cand, cand_left = small[:, 512:768], small[:, 768:1024]
        best_all = small[:, 1024:1024 + 2 * NSEL]
        eq = w4.take(2 * TOPK * TOPK).rearrange("p (c k m) -> p c k m", c=2, k=TOPK)
        part = [small[:, n * P:(n + 1) * P].bitcast(BF16) for n in range(3)]
        left = [small[:, 512 + n * T:512 + (n + 1) * T] for n in range(2)]
        hots = small[:, 0:1024].bitcast(BF16).rearrange("p (b t n i) -> p b t n i", b=2, t=2, n=4)
        iota_bf = small[:, 1024:1024 + P // 2].bitcast(BF16)
        idx_ps = [psum[:, 5 * 512 + n * T:5 * 512 + (n + 1) * T] for n in range(6)]
        W = arena[:, :].rearrange("p (c t) -> p c t", c=NK)

        xhi, xlo = (xr[:, n * KC * L:(n + 1) * KC * L].rearrange("p (k t) -> p k t", k=KC) for n in range(2))
        yhi, ylo = (xr[:, n * KC * T:(n + 1) * KC * T].rearrange("p (k t) -> p k t", k=KC) for n in range(2))
        Whi = [xr[:, n * 2 * T:n * 2 * T + T] for n in range(2)]
        Wlo = [xr[:, n * 2 * T + T:(n + 1) * 2 * T] for n in range(2)]

        def f(ap):
            return ap.bitcast(F32)

        landed = [sem(f"half_landed{s}") for s in range(4)]
        hi_done, lo_done, half_done = sem("hi_done"), sem("lo_done"), sem("half_multiplied")
        bank_free = sem("bank_free")
        loaded, x_loaded = sem("constants_loaded"), sem("x_loaded")
        sq_done, ms_done, std_done = sem("squares_done"), sem("mean_square_done"), sem("std_done")
        normed, split_hi, split_lo = sem("normed"), sem("x_hi_done"), sem("x_lo_done")
        forget_ps, forget_z, forget_e = sem("forget_logits"), sem("forget_z"), sem("forget_ln")
        forget_abs, cum_done, cum_moved, lam_dots, lam_exp = (
            sem("forget_abs"), sem("cum_done"), sem("cum_moved"), sem("lambda_dots"), sem("lambda_exp"))
        dve_s, act_s = sem("vector_chain"), sem("scalar_chain")
        head_ms, head_std, head_normed = sem("head_mean_square"), sem("head_std"), sem("head_normed")
        rot_done, rope_c, roped = sem("rope_swapped"), sem("rope_cos_part"), sem("roped")
        cum_fixed, scored, masked, exped = sem("cum_rows_fixed"), sem("scored"), sem("masked"), sem("exponentials")
        prob_ready, vt_done, v_ready = sem("probabilities"), sem("v_transposed"), sem("v_ready")
        pt_done, pt_ready, pv_done, o_ready = sem("p_transposed"), sem("p_ready"), sem("pv_done"), sem("heads_out")
        sig_done, key_scores, scores_sb, scores_dve = (
            sem("sigmoids"), sem("key_scores"), sem("scores_tile0"), sem("scores_tile1"))
        rows_ps, rows_act, rows_dve, rows_out = (
            sem("h1_rows_psum"), sem("h1_rows_tile0"), sem("h1_rows_tile1"), sem("h1_rows_stored"))
        sc_ready, sc_taken, best_sub, best_exp, chosen, choice_ps = (
            sem("head_scores_ready"), sem("head_scores_taken"), sem("best_less_max"), sem("best_exp"), sem("chosen"),
            sem("choice_transposed"))
        const_used, ones_early, ones_late = sem("constants_used"), sem("early_ones_set"), sem("late_ones_set")
        hot, gate_ps, gated, gelu_done = sem("one_hots"), sem("gates_psum"), sem("gates_applied"), sem("gelu_done")
        w_hi, w_lo = sem("expert_weight_hi"), sem("expert_weight_lo")
        rows_back, summed, out_sb, stored = sem("h1_rows_back"), sem("all_summed"), sem("out_in_sbuf"), sem("stored")

        block = ctx.enter_context(nc.Block())

        def hi_half(act, base, k):
            s = k % 4
            act.wait_ge(landed[s], base * 4 + 16 * (k // 4 + 1))
            nc.scalar.activation(whi[:, s * HALF:(s + 1) * HALF], raw[:, s * HALF:(s + 1) * HALF],
                                 ACT.Copy).then_inc(hi_done, 1)

        def lo_half(dve, base, k):
            s = k % 4
            dve.wait_ge(hi_done, base + k + 1)
            nc.vector.tensor_tensor(wlo[:, k % 2 * HALF:(k % 2 + 1) * HALF], raw[:, s * HALF:(s + 1) * HALF],
                                    f(whi[:, s * HALF:(s + 1) * HALF]), ALU.subtract).then_inc(lo_done, 1)

        @block.sync
        def _(sp):
            sp.dma_start(xT.rearrange("p k t -> p (k t)"), x_t).then_inc(x_loaded, 16)
            sp.dma_start(c_sb, consts).then_inc(loaded, 16)
            sp.dma_start(p_sb, params).then_inc(loaded, 16)

            def load(h, s):
                sp.dma_start(raw[:, s * HALF:(s + 1) * HALF], stream[ds(h, 1), :, :].rearrange("a p n -> (a p) n")
                             ).then_inc(landed[s], 16)

            def load_part(first, end):
                for s in range(4):
                    load(first + s, s)
                with sp.Fori(0, (end - first) // 4 - 1) as i:
                    for s in range(4):
                        sp.wait_ge(lo_done, i * 4 + (first + s + 1))
                        load(i * 4 + (first + 4 + s), s)

            load_part(0, 2 * BLOCKS)
            for s in range(4):
                sp.wait_ge(lo_done, 2 * BLOCKS - 3 + s)
                sp.dma_start(raw[:, s * HALF:(s + 1) * HALF],
                             h1_rows[:, s * HALF:(s + 1) * HALF]).then_inc(rows_back, 16)
            for n in range(8):
                sp.wait_ge(out_sb, n + 1)
                b, q = n // 4, n % 4
                sp.dma_start(out[b * P:(b + 1) * P, q * 512:(q + 1) * 512],
                             arena[:, n * 512:(n + 1) * 512]).then_inc(stored, 16)
            sp.wait_ge(stored, 128)
            sp.wait_ge(rows_out, 16)

        @block.tensor
        def _(pe):
            mm = nc.tensor.matmul

            def mul_half(base, k, acc, hi, lo, start, stop):
                s = k % 4
                pe.wait_ge(hi_done, base + k + 1)
                for c in range(8):
                    w = whi[:, s * HALF + c * P:s * HALF + (c + 1) * P]
                    mm(acc, w, hi[c], start=start and c == 0, stop=False)
                    mm(acc, w, lo[c], start=False, stop=False)
                pe.wait_ge(lo_done, base + k + 1)
                s = k % 2
                for c in range(8):
                    last = mm(acc, wlo[:, s * HALF + c * P:s * HALF + (c + 1) * P], hi[c],
                              start=False, stop=stop and c == 7)
                last.then_inc(half_done, 1)

            def mul_block(base, k, b_free, acc, hi, lo):
                pe.wait_ge(bank_free, b_free)
                mul_half(base, k, acc, hi[0:8], lo[0:8], True, False)
                mul_half(base, k + 1, acc, hi[8:16], lo[8:16], False, True)

            pe.wait_ge(loaded, 32)
            for k in range(KC):
                if k % 4 == 0:
                    pe.wait_ge(sq_done, k // 4 + 1)
                last = mm(bank(7, 0, L), C["mean2048"], hn[:, k, :], start=k == 0, stop=k == KC - 1)
            last.then_inc(ms_done, 1)
            for k in range(KC):
                pe.wait_ge(normed, k + 1)
                last = mm(psum[0:HEADS, 6 * 512:6 * 512 + L], wf[:, k, :], hn[:, k, :], start=k == 0, stop=k == KC - 1)
            last.then_inc(forget_ps, 1)
            pe.wait_ge(split_lo, 4)

            kv = ([xhi[:, k, :] for k in range(KC)], [xlo[:, k, :] for k in range(KC)])
            qg = ([xhi[:, k, META:L] for k in range(KC)], [xlo[:, k, META:L] for k in range(KC)])
            with pe.Fori(0, HEADS) as i:
                def piece(name, a=0, w=None):
                    at, n = QK_AT[name]
                    return qk[:, at + a:at + (n if w is None else a + w)]

                def sq(name):
                    at, n = QK_AT[name]
                    return qk_sq[:, at:at + n]

                for p in range(PER_HEAD):
                    wide = p in (1, 3, 4, 5)
                    hi, lo = kv if wide else qg
                    mul_block(i * 20, 2 * p, i * PER_HEAD + p + 1, bank(p % 2, 0, L if wide else T), hi, lo)
                    if p == 2:
                        pe.wait_ge(bank_free, i * PER_HEAD + 4)
                        pe.wait_ge(o_ready, i * 2 + 1)
                        mm(bank(2, 0, T), C["mean64"], sq("dq"), start=True, stop=True)
                        mm(bank(3, 0, L), C["mean64"], sq("dk"), start=True, stop=True).then_inc(head_ms, 1)
                    if p == 4:
                        pe.wait_ge(head_normed, i * 2 + 1)
                        mm(bank(5, 512 - T, T), C["swap"], piece("dq"), start=True, stop=True)
                        mm(bank(6, 0, L), C["swap"], piece("dk"), start=True, stop=True).then_inc(rot_done, 1)
                        pe.wait_ge(bank_free, i * PER_HEAD + 6)
                        mm(bank(2, T, T), C["mean128"], sq("fq"), start=True, stop=True)
                        mm(bank(4, 0, L), C["mean128"], sq("fk"), start=True, stop=True).then_inc(head_ms, 1)
                    if p == 5:
                        pe.wait_ge(roped, i + 1)
                        for c, b in enumerate((3, 6)):
                            r = slice(64 * c, 64 * c + 64)
                            for n, keys in enumerate(KEYS):
                                last = mm(bank(b, n * KEYS[0], keys), piece("dq", n * P, P)[r], piece("dk", 0, keys)[r],
                                          start=True, stop=True)
                        last.then_inc(scored, 1)
                    if p == 6:
                        pe.wait_ge(head_normed, i * 2 + 2)
                        pe.wait_ge(cum_fixed, i + 1)
                        for n, keys in enumerate(KEYS):
                            acc = bank(4, n * KEYS[0], keys)
                            mm(acc, piece("fq", n * P, P), piece("fk", 0, keys), start=True, stop=False)
                            mm(acc, cum_q[0:1, n * P:(n + 1) * P], C["one"][0:1, 0:keys], start=False, stop=False)
                            last = mm(acc, C["one"][0:1, 0:P], cum_k[0:1, 0:keys], start=False, stop=True)
                        last.then_inc(scored, 1)
                    if p in (5, 6):
                        j, b = p - 5, (7, 5)[p - 5]
                        pe.wait_ge(bank_free, i * PER_HEAD + p + 2)
                        nc.tensor.transpose(psum[0:META, b * 512:b * 512 + P], vT[j][:, 0:META], C["ident"])
                        for n in range(2):
                            last = nc.tensor.transpose(bank(b, P + n * P, P), vT[j][:, META + n * P:META + (n + 1) * P],
                                                       C["ident"])
                        last.then_inc(vt_done, 1)
                    if p in (7, 8):
                        j, b = p - 7, (3, 4)[p - 7]
                        pe.wait_ge(prob_ready, i * 2 + j + 1)
                        src = prob[0 if j == 0 else 2]
                        for n in range(2):
                            a = n * KEYS[0]
                            nc.tensor.transpose(psum[0:META, b * 512 + n * P:b * 512 + (n + 1) * P],
                                                src[:, a:a + META], C["ident"])
                            nc.tensor.transpose(bank(b, T + n * P, P), src[:, a + META:a + META + P], C["ident"])
                        if j == 0:
                            pe.wait_ge(v_ready, i * 2 + 1)
                        last = nc.tensor.transpose(bank(7, 384, P) if j == 0 else bank(6, 0, P),
                                                   src[:, KEYS[0] + META + P:SC_W], C["ident"])
                        last.then_inc(pt_done, 1)
                    if p in (8, 9):
                        j = p - 8
                        pe.wait_ge(pt_ready, i * 2 + j + 1)
                        pe.wait_ge(o_ready, i * 2 + j + 1)
                        pe.wait_ge(v_ready, i * 2 + j + 1)
                        mm(bank(2, j * T, T), v[j][0:META, 0:P], pT[j][0:META, 0:T], start=True, stop=False)
                        mm(bank(2, j * T, T), v[j][:, P:2 * P], pT[j][:, T:2 * T], start=False, stop=False)
                        mm(bank(2, j * T + P, P), v[j][:, 2 * P:3 * P], pT[j][:, 2 * T:2 * T + P],
                           start=False, stop=True).then_inc(pv_done, 1)

            pe.wait_ge(sq_done, 5)
            for h in range(HEADS):
                last = mm(psum[:, 4 * 512 + h * T:4 * 512 + (h + 1) * T], C["mean128"], o_sq[:, h * T:(h + 1) * T],
                          start=True, stop=True)
            last.then_inc(ms_done, 1)

            pe.wait_ge(split_lo, 6)
            hi, lo = [yhi[:, k, :] for k in range(KC)], [ylo[:, k, :] for k in range(KC)]
            with pe.Fori(0, B_BRANCH // 2) as i:
                for q in range(2):
                    pe.wait_ge(bank_free, i * 2 + (F_BRANCH + q + 1))
                    base = i * 4 + 2 * F_BRANCH
                    mul_half(base, 2 * q, bank(q, 0, T), hi[0:8], lo[0:8], True, True)
                    mul_half(base, 2 * q + 1, bank(2 + q, 0, T), hi[8:16], lo[8:16], True, True)
            pe.wait_ge(split_lo, 10)
            with pe.Fori(0, B_OUT // 2) as i:
                for q in range(2):
                    mul_block(i * 4 + 2 * F_OUT, 2 * q, i * 2 + (F_OUT + q + 1), bank(q, 0, T), hi, lo)
            pe.wait_ge(sq_done, 6)
            for k in range(KC):
                last = mm(bank(7, 0, T), C["mean2048"], h2_sq[:, k, :], start=k == 0, stop=k == KC - 1)
            last.then_inc(ms_done, 1)
            pe.wait_ge(split_lo, 14)
            with pe.Fori(0, B_QUERY // 2) as i:
                for q in range(2):
                    mul_block(i * 4 + 2 * F_QUERY, 2 * q, i * 2 + (F_QUERY + q + 1), bank(q, 0, T), hi, lo)
            pe.wait_ge(bank_free, 2 + F_U)
            for b in range(2):
                for g in range(2 * HEADS):
                    h, r = g % HEADS, slice(64 * (g // HEADS), 64 * (g // HEADS) + 64)
                    last = mm(psum[:, (1 - b) * 2048 + g * NK:(1 - b) * 2048 + (g + 1) * NK],
                              qT[r, h, b * P:(b + 1) * P], C["sub_keys"][r, h * NK:(h + 1) * NK],
                              start=True, stop=True)
                last.then_inc(key_scores, 1)
            for b in range(2):
                pe.wait_ge((scores_sb, scores_dve)[b], 1)
                for k in range(KC):
                    a = (1 - b) * 2048 + k * P
                    last = nc.tensor.transpose(psum[:, a:a + P], h1T[:, k, b * P:(b + 1) * P], C["ident"])
                last.then_inc(rows_ps, 1)
            pe.wait_ge(rows_act, 1)
            pe.wait_ge(rows_dve, 1)

            with pe.Fori(0, B_U // 4) as i:
                for q in range(2):
                    mul_block(i * 4 + 2 * F_U, 2 * q, i * 2 + (F_U + q + 1), bank(q, 0, T), hi, lo)
            pe.wait_ge(chosen, 1)
            for n, src in enumerate((chosen_i[:, 0, :], chosen_i[:, 1, :], chosen_g)):
                for b in range(2):
                    last = nc.tensor.transpose(idx_ps[n][:, b * P:(b + 1) * P], src[:, b * P:(b + 1) * P], C["ident"])
            last.then_inc(choice_ps, 1)

            def gate_pair(i, u):
                pe.wait_ge(hot, i * 4 + (u + 1))
                if u % 2 == 0:
                    pe.wait_ge(gated, i * 2 + (u // 2 + 1))
                for t in range(2):
                    out_ = bank(2 + u // 2 % 2, (2 * (u % 2) + t) * P, P)
                    for n in range(3):
                        last = mm(out_, hots[:, u % 2, t, 0, :], hots[:, u % 2, t, 1 + n, :],
                                  start=n == 0, stop=n == 2)
                last.then_inc(gate_ps, 1)

            def late_block(i, c):
                m = 2 * c
                pe.wait_ge(bank_free, i * 2 + (F_G + c + 1))
                mul_half(i * 4 + 2 * F_G, m, bank(c % 2, 0, T), hi[0:8], lo[0:8], True, False)
                if m:
                    gate_pair(i, m - 1)
                mul_half(i * 4 + 2 * F_G, m + 1, bank(c % 2, 0, T), hi[8:16], lo[8:16], False, True)
                gate_pair(i, m)

            late_block(0, 0)
            late_block(0, 1)
            with pe.Fori(0, B_U // 4 - 1) as i:
                for c in (2, 3):
                    late_block(i, c)
            gate_pair(0, T // 2 - 1)

            def value_block(base, c, w_base, first):
                pe.wait_ge(w_hi, w_base + c + 1)
                for j in range(2):
                    k = 2 * c + j
                    s, s2 = k % 4, k % 2
                    pe.wait_ge(hi_done, base + k + 1)
                    for part, sm_ in ((Whi, w_hi), (Wlo, w_lo)):
                        if part is Wlo:
                            pe.wait_ge(w_lo, w_base + c + 1)
                        for b in range(2):
                            for n in range(2):
                                mm(bank(b * 4 + j * 2 + n), part[c % 2][:, b * P:(b + 1) * P],
                                   whi[:, s * HALF + n * 512:s * HALF + (n + 1) * 512],
                                   start=first and part is Whi, stop=False, skip_group_check=True)
                    pe.wait_ge(lo_done, base + k + 1)
                    for b in range(2):
                        for n in range(2):
                            last = mm(bank(b * 4 + j * 2 + n), Whi[c % 2][:, b * P:(b + 1) * P],
                                      wlo[:, s2 * HALF + n * 512:s2 * HALF + (n + 1) * 512],
                                      start=False, stop=True, skip_group_check=True)
                    last.then_inc(half_done, 1)

            pe.wait_ge(bank_free, 2 + F_V)
            pe.wait_ge(gated, T // 4 + 2)
            value_block(2 * F_V, 0, 0, True)
            value_block(2 * F_V, 1, 0, False)
            with pe.Fori(0, B_V // 2 - 1) as i:
                for q in range(2):
                    value_block(i * 4 + 2 * F_V + 4, q, i * 2 + 2, False)

        @block.scalar
        def _(act):
            A = nc.scalar.activation
            ch = Chain(act, act_s)
            eps = C["eps"]

            act.wait_ge(x_loaded, 16)
            for k in range(0, KC, 4):
                A(hn[:, k:k + 4, :], xT[:, k:k + 4, :], ACT.Square).then_inc(sq_done, 1)
            for k in range(2):
                hi_half(act, 0, k)
            act.wait_ge(ms_done, 1)
            A(rstd0, bank(7, 0, L), ACT.Sqrt, bias=eps).then_inc(std_done, 1)
            act.nop().then_inc(bank_free, 2)
            act.nop().then_inc(o_ready, 1)
            for k in range(4):
                act.wait_ge(normed, 4 * k + 4)
                A(xhi[:, 4 * k:4 * k + 4, :], hn[:, 4 * k:4 * k + 4, :], ACT.Copy).then_inc(split_hi, 1)
            for k in range(2, 4):
                hi_half(act, 0, k)
            z8 = fg[0][0:HEADS, :]
            act.wait_ge(forget_ps, 1)
            A(z8, psum[0:HEADS, 6 * 512:6 * 512 + L], ACT.Identity, bias=C["b_forget"][0:HEADS, :]).then_inc(forget_z, 1)
            act.wait_ge(lam_dots, 1)
            A(scal[:, 4:6], scal[:, 2:4], ACT.Exp).then_inc(lam_exp, 1)
            act.wait_ge(forget_abs, 1)
            ch.link(A(fg[2][0:HEADS, :], fg[1][0:HEADS, :], ACT.Exp))
            A(fg[3][0:HEADS, :], fg[2][0:HEADS, :], ACT.Ln, bias=C["one"][0:HEADS, 0:1]).then_inc(forget_e, 1)
            act.wait_ge(cum_done, 1)
            for h in range(HEADS):
                act.dma_start(cum_rows[0:1, h * L:(h + 1) * L], fg[2][h:h + 1, :]).then_inc(cum_moved, 16)
            act.wait_ge(cum_moved, 16 * HEADS)

            with act.Fori(0, HEADS) as i:
                names = ["dq", "dk", "fq", "fk"]
                for p in range(PER_HEAD):
                    act.wait_ge(half_done, i * 20 + 2 * p + 2)
                    if p < 4:
                        at, n = QK_AT[names[p]]
                        A(qk_raw[:, at:at + n], bank(p % 2, 0, n), ACT.Copy)
                        A(qk_sq[:, at:at + n], bank(p % 2, 0, n), ACT.Square).then_inc(bank_free, 1)
                    elif p < 6:
                        A(vT[p - 4], bank(p % 2, 0, L), ACT.Copy).then_inc(bank_free, 1)
                    else:
                        g = i * 4 + (p - 6)
                        A(gates[:, ds(g, 1), :].rearrange("p a t -> p (a t)"), bank(p % 2, 0, T), ACT.Identity,
                          bias=C["b_gate"][:, ds(g, 1)]).then_inc(bank_free, 1)
                    for j in range(2):
                        hi_half(act, i * 20, 2 * p + 4 + j)
                    if p == 0:
                        A(cum_q[0:1, :], cum_rows[0:1, ds(i * L + META, T)], ACT.Copy)
                        A(cum_k[0:1, :], cum_rows[0:1, ds(i * L, L)], ACT.Copy, scale=-1.0).then_inc(cum_fixed, 1)
                    if p in (2, 4):
                        q, k = (("dq", "dk"), ("fq", "fk"))[p // 2 - 1]
                        act.wait_ge(head_ms, i * 2 + p // 2)
                        at, n = QK_AT[q]
                        A(qk_std[:, at:at + n], bank(2, 0 if p == 2 else T, T), ACT.Sqrt, bias=eps)
                        at, n = QK_AT[k]
                        A(qk_std[:, at:at + n], bank(3 if p == 2 else 4, 0, L), ACT.Sqrt,
                          bias=eps).then_inc(head_std, 1)
                    if p in (5, 6):
                        j, b = p - 5, (7, 5)[p - 5]
                        act.wait_ge(vt_done, i * 2 + j + 1)
                        A(v[j][0:META, 0:P], psum[0:META, b * 512:b * 512 + P], ACT.Copy)
                        A(v[j][:, P:3 * P], bank(b, P, 2 * P), ACT.Copy).then_inc(v_ready, 1)
                        for c in ((0, 1), (2,))[j]:
                            act.wait_ge(masked, i * 3 + c + 1)
                            for n, keys in enumerate(KEYS):
                                s = prob[c][:, n * KEYS[0]:n * KEYS[0] + keys]
                                last = A(s, s, ACT.Exp, scale=-1.0, bias=neg_max[:, 2 * c + n:2 * c + n + 1],
                                         accum_out=zsum[:, 2 * c + n:2 * c + n + 1])
                            last.then_inc(exped, 1)
                    if p in (8, 9):
                        j = p - 8
                        act.wait_ge(pv_done, i * 2 + j + 1)
                        A(oT[:, ds(i, 1), j, :].rearrange("p a t -> p (a t)"), bank(2, j * T, T),
                          ACT.Copy).then_inc(o_ready, 1)

            act.wait_ge(o_ready, 2 * HEADS + 1)
            A(o_sq.rearrange("p (h t) -> p h t", h=HEADS), oT[:, :, 0, :], ACT.Square).then_inc(sq_done, 1)
            A(yhi[:, HEADS:KC, :], oT[:, :, 1, :], ACT.Copy).then_inc(split_hi, 1)
            act.wait_ge(ms_done, 2)
            A(o_std, psum[:, 4 * 512:8 * 512], ACT.Sqrt, bias=eps).then_inc(std_done, 1)
            act.wait_ge(normed, KC + 1)
            A(yhi[:, 0:HEADS, :], oT[:, :, 0, :], ACT.Copy).then_inc(split_hi, 1)
            with act.Fori(0, B_BRANCH // 2) as i:
                for q in range(2):
                    gs = [gates[:, ds(i * 2 + q + KC * n, 1), :].rearrange("p a t -> p (a t)") for n in range(2)]
                    A(gs[0], gs[0], ACT.Sigmoid)
                    A(gs[1], gs[1], ACT.Sigmoid).then_inc(sig_done, 1)
                    act.wait_ge(half_done, i * 4 + (2 * F_BRANCH + 2 * q + 2))
                    for j in range(2):
                        hi_half(act, i * 4 + 2 * F_BRANCH, 2 * q + 4 + j)
            for k in range(4):
                act.wait_ge(bank_free, 2 + F_OUT)
                A(yhi[:, 4 * k:4 * k + 4, :], merged[:, 4 * k:4 * k + 4, :], ACT.Copy).then_inc(split_hi, 1)
            with act.Fori(0, B_OUT // 2) as i:
                for q in range(2):
                    act.wait_ge(half_done, i * 4 + (2 * F_OUT + 2 * q + 2))
                    for j in range(2):
                        hi_half(act, i * 4 + 2 * F_OUT, 2 * q + 4 + j)
            act.wait_ge(bank_free, 2 + F_QUERY)
            A(h2_sq[:, :, :], h1T[:, :, :], ACT.Square).then_inc(sq_done, 1)
            act.wait_ge(ms_done, 3)
            A(rstd2, bank(7, 0, T), ACT.Sqrt, bias=eps).then_inc(std_done, 1)
            for k in range(4):
                act.wait_ge(normed, KC + 1 + 4 * k + 4)
                A(yhi[:, 4 * k:4 * k + 4, :], h2[:, 4 * k:4 * k + 4, :], ACT.Copy).then_inc(split_hi, 1)

            def query(i, q):
                act.wait_ge(half_done, i * 4 + (2 * F_QUERY + 2 * q + 2))
                A(qT[:, ds(i * 2 + q, 1), :].rearrange("p a t -> p (a t)"), bank(q, 0, T),
                  ACT.Copy).then_inc(bank_free, 1)

            with act.Fori(0, B_QUERY // 2) as i:
                for q in range(2):
                    query(i, q)
                    for j in range(2):
                        hi_half(act, i * 4 + 2 * F_QUERY, 2 * q + 4 + j)
            act.wait_ge(key_scores, 1)
            A(st[:, 0:HEADS, :, :].rearrange("p h c n -> p c h n"),
              psum[:, 2048:4096].rearrange("p (c h n) -> p c h n", c=2, h=HEADS), ACT.Copy).then_inc(scores_sb, 1)
            act.wait_ge(rows_ps, 1)
            A(rows[:, 0:D], psum[:, 2048:4096], ACT.Copy).then_inc(rows_act, 1)
            act.wait_ge(rows_act, 1)
            act.wait_ge(rows_dve, 1)
            act.dma_start(h1_rows, rows).then_inc(rows_out, 16)

            def one_weight(chunk):
                return W[:, ds(chunk, 1), :].rearrange("p a t -> p (a t)")

            act.wait_ge(scores_sb, 1)
            act.wait_ge(scores_dve, 1)
            with act.Fori(0, 2 * HEADS) as i:
                act.wait_ge(sc_taken, i + 1)
                A(sc, st[:, ds(i, 1), :, :].rearrange("p a c n -> p (a c) n"), ACT.Copy).then_inc(sc_ready, 1)
                for q in range(4):
                    act.wait_ge(half_done, i * 8 + (2 * F_U + 2 * q + 2))
                    A(one_weight(i * 4 + q), bank(q % 2, 0, T), ACT.Gelu).then_inc(bank_free, 1)
                    for j in range(2):
                        hi_half(act, i * 8 + 2 * F_U, 2 * q + 4 + j)
            act.wait_ge(best_sub, 1)
            A(chosen_g, chosen_g, ACT.Exp).then_inc(best_exp, 1)
            with act.Fori(0, B_U // 4) as i:
                for q in range(2):
                    act.wait_ge(half_done, i * 4 + (2 * F_G + 2 * q + 2))
                    A(bank(q, 0, T), bank(q, 0, T), ACT.Gelu).then_inc(gelu_done, 1)
                    for j in range(2):
                        hi_half(act, i * 4 + 2 * F_G, 2 * q + 4 + j)

            def weight_hi(chunk, q):
                A(Whi[q], one_weight(chunk), ACT.Copy).then_inc(w_hi, 1)

            act.wait_ge(half_done, 2 * F_V)
            act.wait_ge(gated, T // 4 + 2)
            act.wait_ge(bank_free, 2 + F_V)
            for q in range(2):
                weight_hi(q, q)
            with act.Fori(0, B_V // 2 - 1) as i:
                for q in range(2):
                    act.wait_ge(half_done, i * 4 + (2 * F_V + 2 * q + 2))
                    weight_hi(i * 2 + (2 + q), q)
                    for j in range(2):
                        hi_half(act, i * 4 + 2 * F_V, 2 * q + 4 + j)

        @block.gpsimd
        def _(pool):
            a = r_work.a
            pool.wait_ge(rows_out, 16)
            pool.wait_ge(rows_ps, 2)
            nc.gpsimd.memset(arena[:, a:a + SPARE], 1.0).then_inc(ones_early, 1)
            pool.wait_ge(choice_ps, 1)
            pool.wait_ge(const_used, 1)
            nc.gpsimd.memset(arena[:, a + SPARE:NK * T], 1.0).then_inc(ones_late, 1)

        @block.vector
        def _(dve):
            V = nc.vector
            ch = Chain(dve, dve_s)

            dve.wait_ge(loaded, 32)
            for n in range(2):
                a = C["lambdas"][:, n * 128:n * 128 + 64]
                b = C["lambdas"][:, n * 128 + 64:n * 128 + 128]
                last = V.tensor_tensor_reduce(out=lam_t, in0=a, in1=b, scale=1.0, scalar=0.0, op0=ALU.mult,
                                              op1=ALU.add, accum_out=scal[:, 2 + n:3 + n])
                if n == 0:
                    ch.link(last)
            last.then_inc(lam_dots, 1)
            ch.link(V.tensor_scalar(C["g_dq"], C["g_dq"], 64 ** -0.5, None, ALU.mult))
            ch.link(V.tensor_scalar(C["g_fq"], C["g_fq"], 128 ** -0.5, None, ALU.mult))
            ch.link(V.tensor_scalar(C["g_sub"], C["g_sub"], 1.0 - LAM_INIT, None, ALU.mult))
            dve.wait_ge(std_done, 1)
            ch.link(V.reciprocal(rstd0, rstd0))
            for k in range(KC):
                V.scalar_tensor_tensor(hn[:, k, :], xT[:, k, :], C["g_mix"][:, k:k + 1], rstd0, ALU.mult,
                                       ALU.mult).then_inc(normed, 1)
            for k in range(4):
                dve.wait_ge(split_hi, k + 1)
                V.tensor_tensor(xlo[:, 4 * k:4 * k + 4, :], hn[:, 4 * k:4 * k + 4, :], f(xhi[:, 4 * k:4 * k + 4, :]),
                                ALU.subtract).then_inc(split_lo, 1)
            for k in range(2):
                lo_half(dve, 0, k)
            dve.wait_ge(lam_exp, 1)
            ch.link(V.tensor_tensor(scal[:, 6:7], scal[:, 4:5], scal[:, 5:6], ALU.subtract))
            ch.link(V.tensor_scalar(neg_lam, scal[:, 6:7], -1.0, -LAM_INIT, ALU.mult, ALU.add))
            z, a_, e_, l_ = (fg[n][0:HEADS, :] for n in range(4))
            dve.wait_ge(forget_z, 1)
            ch.link(V.tensor_scalar(a_, z, -1.0, None, ALU.mult))
            V.tensor_tensor(a_, a_, z, ALU.min).then_inc(forget_abs, 1)
            dve.wait_ge(forget_e, 1)
            ch.link(V.tensor_scalar(z, z, 0.0, None, ALU.min))
            ch.link(V.tensor_tensor(z, z, l_, ALU.subtract))
            V.tensor_tensor_scan(e_, C["one"][0:HEADS, :], z, 0.0, ALU.mult, ALU.add).then_inc(cum_done, 1)

            with dve.Fori(0, HEADS) as i:
                ch.enter(i, 9)

                def normed_piece(name):
                    at, n = QK_AT[name]
                    return V.scalar_tensor_tensor(qk[:, at:at + n], qk_raw[:, at:at + n], C["g_" + name],
                                                  qk_std[:, at:at + n], ALU.mult, ALU.mult)

                def mask_max(c, b):
                    for n, keys in enumerate(KEYS):
                        a = n * KEYS[0]
                        last = V.tensor_tensor_reduce(out=prob[c][:, a:a + keys], in0=bank(b, a, keys),
                                                      in1=C["mask"][:, a:a + keys], scale=-1.0, scalar=3e38,
                                                      op0=ALU.add, op1=ALU.min,
                                                      accum_out=neg_max[:, 2 * c + n:2 * c + n + 1])
                    last.then_inc(masked, 1)

                for p in range(PER_HEAD):
                    for j in range(2):
                        dve.wait_ge(half_done, i * 20 + 2 * p + j + 1)
                        lo_half(dve, i * 20, 2 * p + j + 2)
                        if (p, j) == (3, 0):
                            dve.wait_ge(head_std, i * 2 + 1)
                            ch.link(V.reciprocal(qk_std[:, 0:T + L], qk_std[:, 0:T + L]))
                        if (p, j) == (3, 1):
                            normed_piece("dq")
                            normed_piece("dk").then_inc(head_normed, 1)
                        if (p, j) == (4, 1):
                            dve.wait_ge(head_normed, i * 2 + 1)
                            dve.wait_ge(rot_done, i + 1)
                            ch.link(V.tensor_tensor(rope_a, psum[:, 6 * 512 - T:6 * 512 + L], C["rope_sin"], ALU.mult))
                            ch.link(V.tensor_tensor(rope_b, qk[:, 0:T + L], C["rope_cos"], ALU.mult))
                            V.tensor_tensor(qk[:, 0:T + L], rope_b, rope_a, ALU.add).then_inc(roped, 1)
                        if (p, j) == (5, 0):
                            dve.wait_ge(head_std, i * 2 + 2)
                            ch.link(V.reciprocal(qk_std[:, T + L:QK_W], qk_std[:, T + L:QK_W]))
                        if (p, j) == (5, 1):
                            normed_piece("fq")
                            normed_piece("fk").then_inc(head_normed, 1)
                            dve.wait_ge(scored, 1)
                            dve.wait_ge(scored, i * 2 + 1)
                            mask_max(0, 3)
                        if (p, j) == (6, 0):
                            mask_max(1, 6)
                        if (p, j) == (6, 1):
                            dve.wait_ge(scored, 2)
                            dve.wait_ge(scored, i * 2 + 2)
                            mask_max(2, 4)
                        if (p, j) == (7, 0):
                            dve.wait_ge(exped, i * 3 + 2)
                            ch.link(V.reciprocal(zinv[:, 0:4], zsum[:, 0:4]))
                            ch.link(V.tensor_scalar(zinv[:, 2:4], zinv[:, 2:4], neg_lam, None, ALU.mult))
                            for n, keys in enumerate(KEYS):
                                s = slice(n * KEYS[0], n * KEYS[0] + keys)
                                ch.link(V.tensor_scalar(prob[1][:, s], prob[1][:, s], zinv[:, 2 + n:3 + n], None,
                                                        ALU.mult))
                                last = V.scalar_tensor_tensor(prob[0][:, s], prob[0][:, s], zinv[:, n:n + 1],
                                                              prob[1][:, s], ALU.mult, ALU.add)
                            last.then_inc(prob_ready, 1)
                        if (p, j) == (7, 1):
                            dve.wait_ge(exped, i * 3 + 3)
                            ch.link(V.reciprocal(zinv[:, 4:6], zsum[:, 4:6]))
                            for n, keys in enumerate(KEYS):
                                s = slice(n * KEYS[0], n * KEYS[0] + keys)
                                last = V.tensor_scalar(prob[2][:, s], prob[2][:, s], zinv[:, 4 + n:5 + n], None, ALU.mult)
                            last.then_inc(prob_ready, 1)
                        if (p, j) in ((7, 1), (8, 1)):
                            c = p - 7
                            dve.wait_ge(pt_done, i * 2 + c + 1)
                            b = (3, 4)[c]
                            V.tensor_copy(pT[c][0:META, 0:T], psum[0:META, b * 512:b * 512 + T])
                            V.tensor_copy(pT[c][:, T:2 * T], bank(b, T, T))
                            V.tensor_copy(pT[c][:, 2 * T:2 * T + P],
                                          bank(7, 384, P) if c == 0 else bank(6, 0, P)).then_inc(pt_ready, 1)
                ch.leave(HEADS)

            dve.wait_ge(split_hi, 5)
            V.tensor_tensor(ylo[:, HEADS:KC, :], oT[:, :, 1, :], f(yhi[:, HEADS:KC, :]), ALU.subtract
                            ).then_inc(split_lo, 1)
            dve.wait_ge(std_done, 2)
            ch.link(V.reciprocal(o_std, o_std))
            V.scalar_tensor_tensor(oT[:, :, 0, :], oT[:, :, 0, :], C["g_sub"],
                                   o_std.rearrange("p (h t) -> p h t", h=HEADS), ALU.mult, ALU.mult
                                   ).then_inc(normed, 1)
            dve.wait_ge(split_hi, 6)
            V.tensor_tensor(ylo[:, 0:HEADS, :], oT[:, :, 0, :], f(yhi[:, 0:HEADS, :]), ALU.subtract
                            ).then_inc(split_lo, 1)
            with dve.Fori(0, B_BRANCH // 2) as i:
                ch.enter(i, 4)
                for q in range(2):
                    for j in range(2):
                        dve.wait_ge(half_done, i * 4 + (2 * F_BRANCH + 2 * q + j + 1))
                        lo_half(dve, i * 4 + 2 * F_BRANCH, 2 * q + j + 2)
                        if j == 0:
                            dve.wait_ge(sig_done, i * 2 + q + 1)
                            dve.wait_ge(bank_free, i * 2 + (F_BRANCH + q + 2))
                        g = gates[:, ds(i * 2 + q + KC * j, 1), :].rearrange("p a t -> p (a t)")
                        ch.link(V.tensor_tensor(br[j], bank(2 * j + q, 0, T), g, ALU.mult))
                    V.tensor_tensor(merged[:, ds(i * 2 + q, 1), :].rearrange("p a t -> p (a t)"), br[0], br[1],
                                    ALU.add).then_inc(bank_free, 1)
                ch.leave(B_BRANCH // 2)
            for k in range(4):
                dve.wait_ge(split_hi, 7 + k)
                V.tensor_tensor(ylo[:, 4 * k:4 * k + 4, :], merged[:, 4 * k:4 * k + 4, :],
                                f(yhi[:, 4 * k:4 * k + 4, :]), ALU.subtract).then_inc(split_lo, 1)
            with dve.Fori(0, B_OUT // 2) as i:
                for q in range(2):
                    for j in range(2):
                        dve.wait_ge(half_done, i * 4 + (2 * F_OUT + 2 * q + j + 1))
                        lo_half(dve, i * 4 + 2 * F_OUT, 2 * q + j + 2)
                    V.tensor_tensor(h1T[:, ds(i * 2 + q, 1), :].rearrange("p a t -> p (a t)"), bank(q, 0, T),
                                    xT[:, ds(i * 2 + q, 1), META:L].rearrange("p a t -> p (a t)"),
                                    ALU.add).then_inc(bank_free, 1)
            dve.wait_ge(std_done, 3)
            ch.link(V.reciprocal(rstd2, rstd2))
            for k in range(KC):
                V.scalar_tensor_tensor(h2[:, k, :], h1T[:, k, :], C["g_peer"][:, k:k + 1], rstd2, ALU.mult,
                                       ALU.mult).then_inc(normed, 1)
            for k in range(4):
                dve.wait_ge(split_hi, 11 + k)
                V.tensor_tensor(ylo[:, 4 * k:4 * k + 4, :], h2[:, 4 * k:4 * k + 4, :],
                                f(yhi[:, 4 * k:4 * k + 4, :]), ALU.subtract).then_inc(split_lo, 1)
            with dve.Fori(0, B_QUERY // 2) as i:
                for q in range(2):
                    for j in range(2):
                        dve.wait_ge(half_done, i * 4 + (2 * F_QUERY + 2 * q + j + 1))
                        lo_half(dve, i * 4 + 2 * F_QUERY, 2 * q + j + 2)
            dve.nop().then_inc(sc_taken, 1)
            dve.nop().then_inc(gated, 2)
            dve.wait_ge(key_scores, 2)
            V.tensor_copy(st[:, HEADS:2 * HEADS, :, :].rearrange("p h c n -> p c h n"),
                          psum[:, 0:2048].rearrange("p (c h n) -> p c h n", c=2, h=HEADS)).then_inc(scores_dve, 1)
            dve.wait_ge(rows_ps, 2)
            V.tensor_copy(rows[:, D:2 * D], psum[:, 0:2048]).then_inc(rows_dve, 1)

            ch.spare = small[:, 1280:1280 + 16]
            with dve.Fori(0, 2 * HEADS) as i:
                ch.enter(i, 15)
                mine = ds(i * TOPK, TOPK)
                for m in range(8):
                    dve.wait_ge(half_done, i * 8 + (2 * F_U + m + 1))
                    lo_half(dve, i * 8 + 2 * F_U, m + 2)
                    if m == 0:
                        dve.wait_ge(sc_ready, i + 1)
                        ch.stand(0)
                        V.max(vals[:, 0, 0:8], sc[:, 0, :])
                        ch.link(V.max(vals[:, 1, 0:8], sc[:, 1, :]), True)
                        V.max_index(idxu[:, 0, 0:8], vals[:, 0, 0:8], sc[:, 0, :])
                    if m == 1:
                        V.max_index(idxu[:, 1, 0:8], vals[:, 1, 0:8], sc[:, 1, :])
                        V.match_replace(sc_left[:, 0, :], vals[:, 0, 0:8], sc[:, 0, :], LOWEST)
                        ch.link(V.match_replace(sc_left[:, 1, :], vals[:, 1, 0:8], sc[:, 1, :], LOWEST), True)
                    if m == 2:
                        V.max(vals[:, 0, 8:16], sc_left[:, 0, :])
                        ch.link(V.max(vals[:, 1, 8:16], sc_left[:, 1, :]), True)
                        V.max_index(idxu[:, 0, 8:16], vals[:, 0, 8:16], sc_left[:, 0, :])
                    if m == 3:
                        V.max_index(idxu[:, 1, 8:16], vals[:, 1, 8:16], sc_left[:, 1, :]).then_inc(sc_taken, 1)
                        dve.wait_ge(sc_taken, i + 2)
                        V.tensor_copy(idxf, idxu)
                        ch.link(V.tensor_tensor(cand.rearrange("p (a b) -> p a b", a=TOPK),
                                                spread(vals[:, 0, :].unsqueeze(2), 2, TOPK),
                                                spread(vals[:, 1, :].unsqueeze(1), 1, TOPK), ALU.add), True)
                    if m == 4:
                        ch.link(V.max(best[:, 0:8], cand), True)
                        V.max_index(ju[:, 0:8], best[:, 0:8], cand)
                        ch.link(V.match_replace(cand_left, best[:, 0:8], cand, LOWEST), True)
                    if m == 5:
                        ch.link(V.max(best[:, 8:16], cand_left), True)
                        ch.link(V.max_index(ju[:, 8:16], best[:, 8:16], cand_left))
                        V.tensor_scalar(jh[:, 0, :], ju, 4, None, ALU.logical_shift_right)
                        ch.link(V.tensor_scalar(jh[:, 1, :], ju, TOPK - 1, None, ALU.bitwise_and))
                    if m == 6:
                        ch.link(V.tensor_copy(jf, jh))
                        ch.link(V.tensor_tensor(eq, spread(jf.unsqueeze(3), 3, TOPK),
                                                spread(spread(C["iota16"].unsqueeze(1).unsqueeze(1), 1, 2), 2, TOPK),
                                                ALU.is_equal))
                    if m == 7:
                        ch.link(V.tensor_tensor(eq, eq, spread(idxf.unsqueeze(2), 2, TOPK), ALU.mult))
                        ch.link(V.tensor_copy(best_all[:, mine], best))
                        for c in range(2):
                            ch.link(V.tensor_reduce(chosen_i[:, c, mine], eq[:, c, :, :], AX.X, ALU.add))
                ch.leave(2 * HEADS)
            best3 = best_all.rearrange("p (i k) -> p i k", k=TOPK)
            gate3 = chosen_g.rearrange("p (i k) -> p i k", k=TOPK)
            V.tensor_tensor(gate3, best3, spread(best3[:, :, 0:1], 2, TOPK), ALU.subtract).then_inc(best_sub, 1)
            dve.wait_ge(best_exp, 1)
            ch.link(V.tensor_reduce(gate_sum[:, 0:2 * HEADS], gate3, AX.X, ALU.add))
            ch.link(V.reciprocal(gate_sum[:, 2 * HEADS:4 * HEADS], gate_sum[:, 0:2 * HEADS]))
            V.tensor_tensor(gate3, gate3, spread(gate_sum[:, 2 * HEADS:4 * HEADS].unsqueeze(2), 2, TOPK),
                            ALU.mult).then_inc(chosen, 1)
            V.tensor_copy(iota_bf, C["iota"]).then_inc(const_used, 1)
            dve.wait_ge(choice_ps, 1)
            rest = idx_ps[2]
            for n in range(3):
                ch.link(V.tensor_copy(part[n], rest))
                if n < 2:
                    ch.link(V.tensor_tensor(left[n], rest, part[n], ALU.subtract))
                    rest = left[n]
                ch.link(V.tensor_copy(idx_ps[3 + n], part[n]))

            def late_slot(i, m):
                dve.wait_ge(half_done, i * 4 + (2 * F_G + m + 1))
                if m >= 2:
                    dve.wait_ge(gate_ps, i * 4 + (m - 1))
                for t in range(2):
                    at = [idx_ps[n][:, ds(i * 8 + (2 * m + t), 1)] for n in (0, 1, 3, 4, 5)]
                    row = hots[:, m % 2, t, :, :]
                    V.tensor_scalar(row[:, 0, :], iota_bf, at[0], None, ALU.is_equal)
                    for n in range(3):
                        last = V.tensor_scalar(row[:, 1 + n, :], iota_bf, at[1], at[2 + n], ALU.is_equal, ALU.mult)
                last.then_inc(hot, 1)
                lo_half(dve, i * 4 + 2 * F_G, m + 2)
                if m % 2 == 0 and m:
                    apply_gelu(i, m // 2 - 1)
                if m % 2 and m > 1:
                    apply_gates(i, (m - 3) // 2)

            def apply_gates(i, n):
                dve.wait_ge(gate_ps, i * 4 + (2 * n + 2))
                dve.wait_ge(bank_free, i * 2 + (2 + F_G + n + 1))
                w = W[:, :, ds(i * 8 + 4 * n, 4)].rearrange("p c t -> p t c")
                V.tensor_tensor(w, w, bank(2 + n % 2).rearrange("p (t c) -> p t c", t=4), ALU.mult).then_inc(gated, 1)

            def apply_gelu(i, c):
                dve.wait_ge(gelu_done, i * 2 + (c + 1))
                dve.wait_ge(gated, i * 2 + (c + 2))
                w = W[:, ds(i * 2 + (B_U // 2 + c), 1), :].rearrange("p a t -> p (a t)")
                V.tensor_tensor(w, w, bank(c % 2, 0, T), ALU.mult).then_inc(bank_free, 1)

            for m in range(4):
                if m == 2:
                    dve.wait_ge(ones_early, 1)
                    dve.wait_ge(ones_late, 1)
                late_slot(0, m)
            with dve.Fori(0, B_U // 4 - 1) as i:
                for m in range(4, 8):
                    late_slot(i, m)
            apply_gelu(0, B_U // 2 - 1)
            apply_gates(0, T // 4 - 1)

            def weight_lo(chunk, q, n):
                dve.wait_ge(w_hi, n)
                V.tensor_tensor(Wlo[q], W[:, ds(chunk, 1), :].rearrange("p a t -> p (a t)"), f(Whi[q]),
                                ALU.subtract).then_inc(w_lo, 1)

            dve.wait_ge(gated, T // 4 + 2)
            for q in range(2):
                weight_lo(q, q, q + 1)
            with dve.Fori(0, B_V // 2 - 1) as i:
                for q in range(2):
                    dve.wait_ge(half_done, i * 4 + (2 * F_V + 2 * q + 1))
                    lo_half(dve, i * 4 + 2 * F_V, 2 * q + 2)
                    dve.wait_ge(half_done, i * 4 + (2 * F_V + 2 * q + 2))
                    lo_half(dve, i * 4 + 2 * F_V, 2 * q + 3)
                    weight_lo(i * 2 + (2 + q), q, i * 2 + (3 + q))
            for j in range(2):
                dve.wait_ge(half_done, 2 * BLOCKS - 4 + j + 1)
                lo_half(dve, 2 * BLOCKS - 4, j + 2)
            dve.wait_ge(rows_back, 64)
            for n in range(8):
                b, q = n // 4, n % 4
                dve.wait_ge(half_done, 2 * BLOCKS)
                V.tensor_tensor(arena[:, n * 512:(n + 1) * 512], bank(n), raw[:, n * 512:(n + 1) * 512],
                                ALU.add).then_inc(out_sb, 1)


def lay_out(inputs):
    w_in = inputs["w_in"][0]
    n = HEADS * P
    cuts = np.cumsum([0, n, n, n, n, n, n, HEADS, D, D])
    dq, dk, dv, fq, fk, fv, wf, ga, gb = (w_in[:, a:b] for a, b in zip(cuts[:-1], cuts[1:]))
    gate_cols = np.concatenate([ga, gb], 1)
    order = []
    for h in range(HEADS):
        s = slice(h * P, (h + 1) * P)
        order += [dq[:, s], dk[:, s], fq[:, s], fk[:, s], dv[:, s], fv[:, s], gate_cols[:, h * 4 * P:(h + 1) * 4 * P]]
    branch = np.concatenate([inputs["w_branch_diff"][0], inputs["w_branch_fox"][0]], 0)
    cols = np.concatenate(order + [branch, inputs["w_out"][0], inputs["peer_w_query"][0]], 1)
    first = cols.reshape(KC, P, F_U, P).transpose(2, 1, 0, 3).reshape(F_U, P, D)
    u = inputs["peer_expert_u"][0].reshape(P, NK, KC, P).transpose(1, 3, 2, 0).reshape(B_U, P, D)
    v = inputs["peer_expert_v"][0].reshape(P, NK, D).transpose(1, 0, 2)
    stream = np.empty((BLOCKS, 2, P, HALF), np.float32)
    for at, part in ((0, first), (F_U, u), (F_V, v)):
        stream[at:at + len(part)] = part.reshape(len(part), P, 2, HALF).transpose(0, 2, 1, 3)
    stream = stream.reshape(2 * BLOCKS, P, HALF)

    tokens = np.concatenate([inputs["meta_tokens"], inputs["x"][0]], 0)
    x_t = np.ascontiguousarray(tokens.T.reshape(KC, P, L).transpose(1, 0, 2).reshape(P, KC * L))

    at, width = columns(PARAMS)
    params = np.zeros((P, width), np.float32)

    def put(name, v):
        a, w = at[name]
        params[0:v.shape[0], a:a + w] = v

    put("g_mix", inputs["norm_mix_g"][0].reshape(KC, P).T)
    put("g_peer", inputs["norm_peer_g"][0].reshape(KC, P).T)
    put("b_gate", inputs["b_gate"][0].reshape(2 * KC, P).T)
    put("g_dq", np.tile(inputs["diff_q_norm_g"][0], 2)[:, None])
    put("g_dk", np.tile(inputs["diff_k_norm_g"][0], 2)[:, None])
    put("g_fq", inputs["fox_q_norm_g"][0][:, None])
    put("g_fk", inputs["fox_k_norm_g"][0][:, None])
    put("g_sub", inputs["diff_subln_g"][0][:, None])
    put("b_forget", inputs["b_forget"][0][:, None])
    lam = np.concatenate([inputs[n][0] for n in ("lambda_q1", "lambda_k1", "lambda_q2", "lambda_k2")])
    put("lambdas", np.broadcast_to(lam, (P, 256)))
    put("w_forget", wf.reshape(KC, P, HEADS).transpose(1, 0, 2).reshape(P, KC * HEADS))
    put("sub_keys", inputs["peer_sub_keys"][0].transpose(1, 3, 0, 2).reshape(P, HEADS * NK))
    return {"stream": stream, "x_t": x_t, "params": params, "consts": shape_constants()}


def kernel(**inputs):
    import concourse.bacc as bacc
    from concourse.bass_utils import run_bass_kernel_spmd

    inputs = {k: np.asarray(v) for k, v in inputs.items()}
    arrays = lay_out(inputs)
    nc = bacc.Bacc("TRN2", target_bir_lowering=False, num_devices=1)
    aps = {n: nc.dram_tensor(n, a.shape, F32, kind="ExternalInput").ap() for n, a in arrays.items()}
    h1_rows = nc.dram_tensor("h1_rows", (P, 2 * D), F32, kind="Internal").ap()
    out = nc.dram_tensor("out", (T, D), F32, kind="ExternalOutput").ap()
    hybrid_layer(nc, aps["stream"], aps["x_t"], aps["params"], aps["consts"], h1_rows, out)
    r = run_bass_kernel_spmd(nc, [arrays], core_ids=[0])
    return r.results[0]["out"].reshape(1, T, D)
```

```python
import numpy as np
from contextlib import ExitStack

import concourse.bass as bass
from concourse import mybir

F32 = mybir.dt.float32
F32R = mybir.dt.float32r
U32 = mybir.dt.uint32
BF16 = mybir.dt.bfloat16
ACT = mybir.ActivationFunctionType
ALU = mybir.AluOpType
AX = mybir.AxisListType
ds = bass.ds

P = 128
D = 2048
KC = D // P
META = 16
T = 256
L = META + T
HEADS = 8
PER_HEAD = 10
NK = 128
TOPK = 16
NSEL = HEADS * TOPK
EPS = 1e-6
LAM_INIT = 0.2
HALF = 1024
NEG = -1e30
LOWEST = -3.0e38

B_W_IN = HEADS * PER_HEAD
B_BRANCH, B_OUT, B_QUERY, B_U, B_V = KC, KC, HEADS, NK, NK
F_BRANCH = B_W_IN
F_OUT = F_BRANCH + B_BRANCH
F_QUERY = F_OUT + B_OUT
F_U = F_QUERY + B_QUERY
F_V = F_U + B_U
BLOCKS = F_V + B_V
PIECES = [(0, 2), (2, 4), (4, 8), (8, 12), (12, 16)]
STARTS = {a: n for n, (a, b) in enumerate(PIECES)}
F_G = F_U + B_U // 2

QK_AT = {"dq": (0, T), "dk": (T, L), "fq": (T + L, T), "fk": (2 * T + L, L)}
QK_W = 2 * (T + L)
KEYS = (META + P, META + 2 * P)
SC_W = sum(KEYS)

CONSTS = [("mean2048", P), ("eps", 1), ("rope_cos", T + L), ("rope_sin", T + L), ("mask", SC_W), ("mean64", P),
          ("mean128", P), ("swap", P), ("ident", P), ("iota", P), ("iota16", TOPK), ("one", 1), ("rows01", 3)]
FIRST_CONSTS = P + 1
PARAMS = [("g_mix", KC), ("g_peer", KC), ("b_gate", 2 * KC), ("g_dq", 1), ("g_dk", 1), ("g_fq", 1), ("g_fk", 1),
          ("g_sub", 1), ("b_forget", 1), ("lambdas", 256), ("w_forget", KC * HEADS), ("sub_keys", HEADS * NK)]


def columns(table):
    at, out = 0, {}
    for name, w in table:
        out[name] = (at, w)
        at += w
    return out, at


def shape_constants():
    at, width = columns(CONSTS)
    c = np.zeros((P, width), np.float32)

    def put(name, v):
        a, w = at[name]
        c[:, a:a + w] = v

    rot = 16
    inv = (np.float32(500000.0) ** (-np.arange(0, rot, 2, dtype=np.float32) / np.float32(rot))).astype(np.float32)
    ang = (np.arange(L, dtype=np.float32)[:, None] * inv[None, :]).astype(np.float32)
    cos, sin = np.cos(ang).T, np.sin(ang).T
    cc, ss = np.ones((P, L), np.float32), np.zeros((P, L), np.float32)
    swap = np.zeros((P, P), np.float32)
    for b in (0, 64):
        cc[b:b + 8], cc[b + 8:b + 16] = cos, cos
        ss[b:b + 8], ss[b + 8:b + 16] = -sin, sin
        for j in range(8):
            swap[b + j + 8, b + j] = 1.0
            swap[b + j, b + j + 8] = 1.0
    put("rope_cos", np.concatenate([cc[:, META:], cc], 1))
    put("rope_sin", np.concatenate([ss[:, META:], ss], 1))
    q, k = np.arange(P)[:, None], np.arange(L)[None, :]
    put("mask", np.concatenate([np.where(k[:, :n] <= q + META + b * P, 0.0, NEG) for b, n in enumerate(KEYS)], 1))
    bd = np.zeros((P, P), np.float32)
    bd[:64, :64] = bd[64:, 64:] = 1.0 / 64
    put("mean64", bd)
    put("mean128", 1.0 / 128)
    put("mean2048", 1.0 / 2048)
    put("swap", swap)
    put("ident", np.eye(P))
    put("iota", np.arange(P)[None, :])
    put("iota16", np.arange(TOPK)[None, :])
    put("eps", EPS)
    put("one", 1.0)
    put("rows01", [[1, 0, 0], [0, 1, -1]] + [[0, 0, 0]] * (P - 2))
    return c


def spread(ap, dim, n):
    shape = list(ap.shape)
    shape[dim] = n
    return ap.broadcast_to(shape)


class Chain:

    def __init__(self, eng, sem):
        self.eng, self.sem, self.base, self.n = eng, sem, 0, 0

    def link(self, ins, before_max=False):
        self.n += 1
        ins.then_inc(self.sem, 1)
        self.eng.wait_ge(self.sem, self.base + self.n)
        if before_max:
            self.stand(self.n)

    def stand(self, n):
        self.eng.memset(self.spare[:, n:n + 1], 0.0)

    def enter(self, i, per_turn):
        self.start = self.base + self.n
        self.base, self.n, self.per_turn = self.start + i * per_turn, 0, per_turn

    def leave(self, turns):
        assert self.n == self.per_turn, (self.n, self.per_turn)
        self.base, self.n = self.start + turns * self.per_turn, 0


def hybrid_layer(nc, stream, x_t, params, consts, h1_rows, out):
    with ExitStack() as ctx:
        def sb(name, cols, dt=F32):
            return ctx.enter_context(nc.sbuf_tensor(name, [P, cols], dt))

        def sem(name):
            return ctx.enter_context(nc.semaphore(name))

        arena = sb("arena", NK * T)
        xr = sb("xr", 2 * KC * L, F32R)
        raw = sb("raw", 4 * HALF)
        whi = sb("whi", 4 * HALF, F32R)
        wlo = sb("wlo", 2 * HALF, F32R)
        small = sb("small", 1472)
        psum = ctx.enter_context(nc.psum_tensor("psum", [P, 8 * 512], F32))

        def bank(b, a=0, w=512):
            return psum[:, b * 512 + a:b * 512 + a + w]

        class Region:

            def __init__(self, a, b):
                self.a, self.b, self.first = a, b, a

            def take(self, w):
                a = self.a
                self.a += w
                assert self.a <= self.b, (self.a, self.b)
                return arena[:, a:a + w]

            def again(self):
                return Region(self.first, self.b)

            def sub(self, w):
                a = self.a
                self.take(w)
                return Region(a, a + w)

        MID = NK * T // 2
        low, high = Region(0, MID), Region(MID, NK * T)
        c_at, c_w = columns(CONSTS)
        p_at, p_w = columns(PARAMS)
        xT = low.take(KC * L).rearrange("p (k t) -> p k t", k=KC)
        r_gates = low.sub(2 * KC * T)
        p_sb = low.take(p_w)
        scal = low.take(16)
        r_low = low.sub(MID - low.a)
        r_work = high.sub(NK * T - MID - c_w - 2 * HEADS * T)
        r_o = high.sub(2 * HEADS * T)
        c_sb = high.take(c_w)
        C = {n: c_sb[:, a:a + w] for n, (a, w) in c_at.items()}
        C.update({n: p_sb[:, a:a + w] for n, (a, w) in p_at.items()})
        wf = C["w_forget"].rearrange("p (k h) -> p k h", k=KC)
        neg_lam = scal[:, 0:1]
        gates = r_gates.again().take(2 * KC * T).rearrange("p (g t) -> p g t", g=2 * KC)
        oT = r_o.again().take(2 * HEADS * T).rearrange("p (h j t) -> p h j t", h=HEADS, j=2)

        w0 = r_work.again()
        hn = w0.take(KC * L).rearrange("p (k t) -> p k t", k=KC)
        rstd0 = w0.take(L)
        fg = [w0.take(L) for _ in range(4)]
        lam_t = w0.take(64)
        sums = [small[:, n * L:(n + 1) * L] for n in range(4)]
        wf_hi, wf_lo = (whi[:, 3 * HALF + n * P:3 * HALF + (n + 1) * P] for n in range(2))
        w1 = r_work.again()
        qk_raw = w1.take(QK_W)
        qk_sq = w1.take(QK_W)
        qk_std = w1.take(QK_W)
        qk = w1.take(QK_W)
        assert w1.a <= r_work.a + KC * L
        w1.a = w0.a
        rope_a, rope_b = w1.take(T + L), qk_sq[:, 0:T + L]
        v = [w1.take(384) for _ in range(2)]
        cum_rows = r_low.again().take(HEADS * L)
        o_sq, o_std = small[:, T + L:2 * T + L], small[:, 2 * T + L + SC_W:3 * T + L + SC_W]
        cum_q, cum_k = small[:, 0:T], w1.take(L)
        vT = [w1.take(L), small[:, T:T + L]]
        prob = [w1.take(SC_W) for _ in range(2)] + [small[:, 2 * T + L:2 * T + L + SC_W]]
        pT = [w1.take(640) for _ in range(2)]
        sm = w1.take(24)
        neg_max, zsum, zinv = sm[:, 0:6], sm[:, 6:12], sm[:, 12:18]
        w2 = r_work.again()
        merged = w2.take(KC * T).rearrange("p (k t) -> p k t", k=KC)
        h1T = w2.take(KC * T).rearrange("p (k t) -> p k t", k=KC)
        br = [w2.take(T) for _ in range(2)]
        h2 = merged
        rows = r_o.again().take(2 * D)
        w3 = r_gates.again()
        h2_sq = w3.take(KC * T).rearrange("p (k t) -> p k t", k=KC)
        rstd2 = w3.take(T)
        qT = w3.take(HEADS * T).rearrange("p (h t) -> p h t", h=HEADS)
        st = r_work.again().take(4 * HEADS * NK).rearrange("p (i c n) -> p i c n", i=2 * HEADS, c=2)
        SPARE = 2 * KC * T
        w4 = Region(r_work.a + SPARE, r_work.b)
        chosen_i = w4.take(2 * 2 * NSEL).rearrange("p (c s) -> p c s", c=2)
        chosen_g = w4.take(2 * NSEL)
        gate_sum = w4.take(4 * HEADS)
        vals = w4.take(2 * TOPK).rearrange("p (c m) -> p c m", c=2)
        idxf = w4.take(2 * TOPK).rearrange("p (c m) -> p c m", c=2)
        idxu = w4.take(2 * TOPK).bitcast(U32).rearrange("p (c m) -> p c m", c=2)
        best = w4.take(TOPK)
        ju = w4.take(TOPK).bitcast(U32)
        jh = w4.take(2 * TOPK).bitcast(U32).rearrange("p (c m) -> p c m", c=2)
        jf = w4.take(2 * TOPK).rearrange("p (c m) -> p c m", c=2)
        sc = small[:, 0:2 * NK].rearrange("p (c n) -> p c n", c=2)
        sc_left = small[:, 256:256 + 2 * NK].rearrange("p (c n) -> p c n", c=2)
        cand, cand_left = small[:, 512:768], small[:, 768:1024]
        best_all = small[:, 1024:1024 + 2 * NSEL]
        eq = w4.take(2 * TOPK * TOPK).rearrange("p (c k m) -> p c k m", c=2, k=TOPK)
        part = [small[:, n * P:(n + 1) * P].bitcast(BF16) for n in range(3)]
        left = [small[:, 512 + n * T:512 + (n + 1) * T] for n in range(2)]
        hots = small[:, 0:1024].bitcast(BF16).rearrange("p (b t n i) -> p b t n i", b=2, t=2, n=4)
        iota_bf = small[:, 1024:1024 + P // 2].bitcast(BF16)
        row2 = small[:, 1088:1088 + 2 * P].bitcast(BF16).rearrange("p (b t i) -> p b t i", b=2, t=2)
        idx_ps = [psum[:, 5 * 512 + n * T:5 * 512 + (n + 1) * T] for n in range(4)]
        gate_sb = [xr[:, 2 * KC * T + n * T:2 * KC * T + (n + 1) * T] for n in range(2)]
        W = arena[:, :].rearrange("p (c t) -> p c t", c=NK)

        xhi, xlo = (xr[:, n * KC * L:(n + 1) * KC * L].rearrange("p (k t) -> p k t", k=KC) for n in range(2))
        yhi, ylo = (xr[:, n * KC * T:(n + 1) * KC * T].rearrange("p (k t) -> p k t", k=KC) for n in range(2))
        Whi = [xr[:, n * 2 * T:n * 2 * T + T] for n in range(2)]
        Wlo = [xr[:, n * 2 * T + T:(n + 1) * 2 * T] for n in range(2)]

        OUT_ORDER = (0, 1, 4, 5, 2, 3, 6, 7)
        SCORES = ((6, 0), (2, 4))

        def f(ap):
            return ap.bitcast(F32)

        landed = [sem(f"half_landed{s}") for s in range(4)]
        hi_done, lo_done, half_done = sem("hi_done"), sem("lo_done"), sem("half_multiplied")
        bank_free = sem("bank_free")
        loaded, x_loaded = sem("constants_loaded"), [sem(f"x_loaded{n}") for n in range(4)]
        first_loaded, params_loaded, sums_done = sem("first_constants_loaded"), sem("params_loaded"), sem("sums_done")
        wf_split, wf_rest = sem("forget_weights_hi"), sem("forget_weights_lo")
        sq_done, ms_done, std_done = sem("squares_done"), sem("mean_square_done"), sem("std_done")
        normed, split_hi, split_lo = sem("normed"), sem("x_hi_done"), sem("x_lo_done")
        forget_ps, forget_z, forget_e = sem("forget_logits"), sem("forget_z"), sem("forget_ln")
        forget_abs, cum_done, cum_moved, lam_dots, lam_exp = (
            sem("forget_abs"), sem("cum_done"), sem("cum_moved"), sem("lambda_dots"), sem("lambda_exp"))
        dve_s, act_s = sem("vector_chain"), sem("scalar_chain")
        head_ms, head_std, head_normed = sem("head_mean_square"), sem("head_std"), sem("head_normed")
        rot_done, roped = sem("rope_swapped"), sem("roped")
        cum_fixed, scored, masked, exped = sem("cum_rows_fixed"), sem("scored"), sem("masked"), sem("exponentials")
        prob_ready, vt_done, v_ready = sem("probabilities"), sem("v_transposed"), sem("v_ready")
        pt_done, pt_ready, pv_done, o_ready = sem("p_transposed"), sem("p_ready"), sem("pv_done"), sem("heads_out")
        sig_done, key_scores, scores_sb, scores_dve = (
            sem("sigmoids"), sem("key_scores"), sem("scores_tile0"), sem("scores_tile1"))
        rows_ps, rows_act, rows_out = sem("h1_rows_psum"), sem("h1_rows_in_sbuf"), sem("h1_rows_stored")
        sc_ready, sc_taken, best_sub, best_exp, chosen, choice_ps = (
            sem("head_scores_ready"), sem("head_scores_taken"), sem("best_less_max"), sem("best_exp"), sem("chosen"),
            sem("choice_transposed"))
        const_used, ones_early, ones_late = sem("constants_used"), sem("early_ones_set"), sem("late_ones_set")
        o_ms, o_std_done, heads_normed = sem("head_out_mean_square"), sem("head_out_std"), sem("head_out_normed")
        row_ready, gate_split = sem("one_hot_rows"), sem("gate_parts")
        first_weights = sem("first_weights_done")
        hot, gate_ps, gated, gelu_done = sem("one_hots"), sem("gates_psum"), sem("gates_applied"), sem("gelu_done")
        w_hi, w_lo = sem("expert_weight_hi"), sem("expert_weight_lo")
        rows_back = [sem(f"h1_rows_back{n}") for n in range(4)]
        out_sb, stored = sem("out_in_sbuf"), sem("stored")

        block = ctx.enter_context(nc.Block())

        def hi_half(act, base, k):
            s = k % 4
            act.wait_ge(landed[s], base * 4 + 16 * (k // 4 + 1))
            nc.scalar.activation(whi[:, s * HALF:(s + 1) * HALF], raw[:, s * HALF:(s + 1) * HALF],
                                 ACT.Copy).then_inc(hi_done, 1)

        def lo_half(dve, base, k):
            s = k % 4
            dve.wait_ge(hi_done, base + k + 1)
            nc.vector.tensor_tensor(wlo[:, k % 2 * HALF:(k % 2 + 1) * HALF], raw[:, s * HALF:(s + 1) * HALF],
                                    f(whi[:, s * HALF:(s + 1) * HALF]), ALU.subtract).then_inc(lo_done, 1)

        @block.sync
        def _(sp):
            for k in range(0, KC, 4):
                sp.dma_start(xT[:, k:k + 4, :].rearrange("p k t -> p (k t)"),
                             x_t[:, k * L:(k + 4) * L]).then_inc(x_loaded[k // 4], 16)
                if k == 0:
                    sp.dma_start(c_sb[:, 0:FIRST_CONSTS], consts[:, 0:FIRST_CONSTS]).then_inc(first_loaded, 16)

            def load(h, s):
                sp.dma_start(raw[:, s * HALF:(s + 1) * HALF], stream[ds(h, 1), :, :].rearrange("a p n -> (a p) n")
                             ).then_inc(landed[s], 16)

            for s in range(2):
                load(s, s)
            sp.dma_start(p_sb, params).then_inc(params_loaded, 16)
            for s in range(2, 4):
                load(s, s)
            sp.dma_start(c_sb[:, FIRST_CONSTS:], consts[:, FIRST_CONSTS:]).then_inc(loaded, 16)
            with sp.Fori(0, BLOCKS // 2 - 1) as i:
                for s in range(4):
                    sp.wait_ge(lo_done, i * 4 + (s + 1))
                    load(i * 4 + (4 + s), s)
            for s in range(4):
                sp.wait_ge(lo_done, 2 * BLOCKS - 3 + s)
                sp.dma_start(raw[:, s * HALF:(s + 1) * HALF],
                             h1_rows[:, s * HALF:(s + 1) * HALF]).then_inc(rows_back[s], 16)
            for at, n in enumerate(OUT_ORDER):
                sp.wait_ge(out_sb, at + 1)
                b, q = n // 4, n % 4
                sp.dma_start(out[b * P:(b + 1) * P, q * 512:(q + 1) * 512],
                             arena[:, n * 512:(n + 1) * 512]).then_inc(stored, 16)
            sp.wait_ge(stored, 128)
            sp.wait_ge(rows_out, 16)

        @block.tensor
        def _(pe):
            mm = nc.tensor.matmul

            def mul_half(base, k, acc, hi, lo, start, stop, split={}):
                s = k % 4
                pe.wait_ge(hi_done, base + k + 1)
                for c in range(8):
                    if c in split:
                        pe.wait_ge(split_lo, split[c])
                    w = whi[:, s * HALF + c * P:s * HALF + (c + 1) * P]
                    mm(acc, w, hi[c], start=start and c == 0, stop=False)
                    mm(acc, w, lo[c], start=False, stop=False)
                pe.wait_ge(lo_done, base + k + 1)
                s = k % 2
                for c in range(8):
                    last = mm(acc, wlo[:, s * HALF + c * P:s * HALF + (c + 1) * P], hi[c],
                              start=False, stop=stop and c == 7)
                last.then_inc(half_done, 1)

            def mul_block(base, k, b_free, acc, hi, lo, split=None):
                pe.wait_ge(bank_free, b_free)
                first, second = {}, {}
                if split is not None:
                    first, second = ({a - c: split + n + 1 for n, (a, b) in enumerate(PIECES) if c <= a < c + 8}
                                     for c in (0, 8))
                mul_half(base, k, acc, hi[0:8], lo[0:8], True, False, first)
                mul_half(base, k + 1, acc, hi[8:16], lo[8:16], False, True, second)

            pe.wait_ge(first_loaded, 16)
            for n in range(4):
                pe.wait_ge(sums_done, n + 1)
                last = mm(bank(7, 0, L), C["mean2048"], sums[n], start=n == 0, stop=n == 3)
            last.then_inc(ms_done, 1)
            pe.wait_ge(wf_rest, 1)
            for k in range(KC):
                if k in STARTS:
                    pe.wait_ge(split_lo, STARTS[k] + 1)
                for n, (w, x) in enumerate(((wf_hi, xhi), (wf_hi, xlo), (wf_lo, xhi))):
                    last = mm(psum[0:HEADS, 6 * 512:6 * 512 + L], w[:, k * HEADS:(k + 1) * HEADS], x[:, k, :],
                              start=k == 0 and n == 0, stop=k == KC - 1 and n == 2)
            last.then_inc(forget_ps, 1)
            pe.wait_ge(loaded, 16)

            kv = ([xhi[:, k, :] for k in range(KC)], [xlo[:, k, :] for k in range(KC)])
            qg = ([xhi[:, k, META:L] for k in range(KC)], [xlo[:, k, META:L] for k in range(KC)])
            with pe.Fori(0, HEADS) as i:
                def piece(name, a=0, w=None):
                    at, n = QK_AT[name]
                    return qk[:, at + a:at + (n if w is None else a + w)]

                def sq(name):
                    at, n = QK_AT[name]
                    return qk_sq[:, at:at + n]

                for p in range(PER_HEAD):
                    wide = p in (1, 3, 4, 5)
                    hi, lo = kv if wide else qg
                    mul_block(i * 20, 2 * p, i * PER_HEAD + p + 1, bank(p % 2, 0, L if wide else T), hi, lo)
                    if p == 2:
                        pe.wait_ge(bank_free, i * PER_HEAD + 4)
                        pe.wait_ge(o_ready, i * 2 + 1)
                        mm(bank(2, 0, T), C["mean64"], sq("dq"), start=True, stop=True)
                        mm(bank(3, 0, L), C["mean64"], sq("dk"), start=True, stop=True).then_inc(head_ms, 1)
                    if p == 4:
                        pe.wait_ge(head_normed, i * 2 + 1)
                        mm(bank(5, 512 - T, T), C["swap"], piece("dq"), start=True, stop=True)
                        mm(bank(6, 0, L), C["swap"], piece("dk"), start=True, stop=True).then_inc(rot_done, 1)
                        pe.wait_ge(bank_free, i * PER_HEAD + 6)
                        mm(bank(2, T, T), C["mean128"], sq("fq"), start=True, stop=True)
                        mm(bank(4, 0, L), C["mean128"], sq("fk"), start=True, stop=True).then_inc(head_ms, 1)
                    if p == 5:
                        pe.wait_ge(roped, i + 1)
                        for c, b in enumerate((3, 6)):
                            r = slice(64 * c, 64 * c + 64)
                            for n, keys in enumerate(KEYS):
                                last = mm(bank(b, n * KEYS[0], keys), piece("dq", n * P, P)[r], piece("dk", 0, keys)[r],
                                          start=True, stop=True)
                        last.then_inc(scored, 1)
                    if p == 6:
                        pe.wait_ge(head_normed, i * 2 + 2)
                        pe.wait_ge(cum_fixed, i + 1)
                        for n, keys in enumerate(KEYS):
                            acc = bank(4, n * KEYS[0], keys)
                            mm(acc, piece("fq", n * P, P), piece("fk", 0, keys), start=True, stop=False)
                            last = mm(acc, cum_q[0:2, n * P:(n + 1) * P], cum_k[0:2, 0:keys], start=False, stop=True)
                        last.then_inc(scored, 1)
                    if p in (5, 6):
                        j, b = p - 5, (7, 5)[p - 5]
                        pe.wait_ge(bank_free, i * PER_HEAD + p + 2)
                        nc.tensor.transpose(psum[0:META, b * 512:b * 512 + P], vT[j][:, 0:META], C["ident"])
                        for n in range(2):
                            last = nc.tensor.transpose(bank(b, P + n * P, P), vT[j][:, META + n * P:META + (n + 1) * P],
                                                       C["ident"])
                        last.then_inc(vt_done, 1)
                    if p in (7, 8):
                        j, b = p - 7, (3, 4)[p - 7]
                        pe.wait_ge(prob_ready, i * 2 + j + 1)
                        src = prob[0 if j == 0 else 2]
                        for n in range(2):
                            a = n * KEYS[0]
                            nc.tensor.transpose(psum[0:META, b * 512 + n * P:b * 512 + (n + 1) * P],
                                                src[:, a:a + META], C["ident"])
                            nc.tensor.transpose(bank(b, T + n * P, P), src[:, a + META:a + META + P], C["ident"])
                        if j == 0:
                            pe.wait_ge(v_ready, i * 2 + 1)
                        last = nc.tensor.transpose(bank(7, 384, P) if j == 0 else bank(6, 0, P),
                                                   src[:, KEYS[0] + META + P:SC_W], C["ident"])
                        last.then_inc(pt_done, 1)
                    if p in (8, 9):
                        j = p - 8
                        pe.wait_ge(pt_ready, i * 2 + j + 1)
                        pe.wait_ge(o_ready, i * 2 + j + 1)
                        pe.wait_ge(v_ready, i * 2 + j + 1)
                        if j:
                            mm(bank(7, 0, T), C["mean128"], o_sq, start=True, stop=True).then_inc(o_ms, 1)
                        mm(bank(2, j * T, T), v[j][0:META, 0:P], pT[j][0:META, 0:T], start=True, stop=False)
                        mm(bank(2, j * T, T), v[j][:, P:2 * P], pT[j][:, T:2 * T], start=False, stop=False)
                        mm(bank(2, j * T + P, P), v[j][:, 2 * P:3 * P], pT[j][:, 2 * T:2 * T + P],
                           start=False, stop=True).then_inc(pv_done, 1)

            hi, lo = [yhi[:, k, :] for k in range(KC)], [ylo[:, k, :] for k in range(KC)]

            def branch_block(i, q, split):
                pe.wait_ge(bank_free, i * 2 + (F_BRANCH + q + 1))
                base = i * 4 + 2 * F_BRANCH
                mul_half(base, 2 * q, bank(2 + q % 2, 0, T), hi[0:8], lo[0:8], True, True, split[0])
                mul_half(base, 2 * q + 1, bank(q % 2, 0, T), hi[8:16], lo[8:16], True, True, split[1])

            branch_block(0, 0, ({0: 6, 2: 7, 4: 8}, {0: 9, 4: 10}))
            branch_block(0, 1, ({}, {}))
            with pe.Fori(0, B_BRANCH // 2 - 1) as i:
                for q in range(2, 4):
                    branch_block(i, q, ({}, {}))

            def h1_square(k, n, start, stop):
                pe.wait_ge(sq_done, n)
                return mm(bank(7, 0, T), C["mean2048"], h2_sq[:, ds(k, 1), :].rearrange("p a t -> p (a t)"),
                          start=start, stop=stop, skip_group_check=True)

            for q in range(2):
                mul_block(2 * F_OUT, 2 * q, F_OUT + q + 1, bank(q, 0, T), hi, lo, None if q else 10)
            h1_square(0, 5, True, False)
            with pe.Fori(0, B_OUT // 2 - 1) as i:
                for q in range(2, 4):
                    mul_block(i * 4 + 2 * F_OUT, 2 * q, i * 2 + (F_OUT + q + 1), bank(q - 2, 0, T), hi, lo)
                    h1_square(i * 2 + (q - 1), i * 2 + (q + 4), False, False)
            h1_square(KC - 1, KC + 4, False, True).then_inc(ms_done, 1)

            def h1_to_rows(b, at, first, end):
                for k in range(first, end):
                    last = nc.tensor.transpose(bank(at, (k - first) * P, P), h1T[:, k, b * P:(b + 1) * P], C["ident"])
                last.then_inc(rows_ps, 1)

            pe.wait_ge(bank_free, 2 + F_QUERY)
            h1_to_rows(1, 0, KC // 2, KC)
            h1_to_rows(0, 2, 0, KC)
            pe.wait_ge(std_done, 2)
            h1_to_rows(1, 6, 0, KC // 2)
            pe.wait_ge(rows_act, 1)
            for q in range(2):
                mul_block(2 * F_QUERY, 2 * q, F_QUERY + q + 1, bank(q, 0, T), hi, lo, None if q else 15)
            with pe.Fori(0, B_QUERY // 2 - 1) as i:
                for q in range(2, 4):
                    mul_block(i * 4 + 2 * F_QUERY, 2 * q, i * 2 + (F_QUERY + q + 1), bank(q - 2, 0, T), hi, lo)
            pe.wait_ge(rows_act, 2)
            pe.wait_ge(bank_free, 2 + F_U)
            for b in range(2):
                for g in range(2 * HEADS):
                    h, r = g % HEADS, slice(64 * (g // HEADS), 64 * (g // HEADS) + 64)
                    last = mm(bank((SCORES[b][g // HEADS]), h * NK, NK),
                              qT[r, h, b * P:(b + 1) * P], C["sub_keys"][r, h * NK:(h + 1) * NK],
                              start=True, stop=True)
                last.then_inc(key_scores, 1)
            pe.wait_ge(scores_sb, 1)

            with pe.Fori(0, B_U // 4) as i:
                for q in range(2):
                    mul_block(i * 4 + 2 * F_U, 2 * q, i * 2 + (F_U + q + 1), bank(q, 0, T), hi, lo)
            def gate_pair(i, u):
                pe.wait_ge(hot, i * 4 + (u + 1))
                if u % 2 == 0:
                    pe.wait_ge(gated, i * 2 + (u // 2 + 1))
                for t in range(2):
                    out_ = bank(2 + u // 2 % 2, (2 * (u % 2) + t) * P, P)
                    for n in range(3):
                        last = mm(out_, hots[:, u % 2, t, 0, :], hots[:, u % 2, t, 1 + n, :],
                                  start=n == 0, stop=n == 2)
                last.then_inc(gate_ps, 1)

            def late_half(i, m):
                c, j = m // 2, m % 2
                if j == 0:
                    pe.wait_ge(bank_free, i * 2 + (F_G + c + 1))
                mul_half(i * 4 + 2 * F_G, m, bank(c % 2, 0, T), hi[8 * j:8 * j + 8], lo[8 * j:8 * j + 8],
                         j == 0, j == 1)

            late_half(0, 0)
            pe.wait_ge(chosen, 1)
            for n, src in enumerate((chosen_i[:, 0, :], chosen_i[:, 1, :], chosen_g)):
                for b in range(2):
                    last = nc.tensor.transpose(idx_ps[n][:, b * P:(b + 1) * P], src[:, b * P:(b + 1) * P], C["ident"])
            last.then_inc(choice_ps, 1)

            late_half(0, 1)
            late_half(0, 2)
            gate_pair(0, 0)
            late_half(0, 3)
            gate_pair(0, 1)
            gate_pair(0, 2)
            with pe.Fori(0, B_U // 4 - 1) as i:
                for m in range(4, 8):
                    late_half(i, m)
                    gate_pair(i, m - 1)
            gate_pair(0, T // 2 - 1)

            def value_block(base, c, w_base, first):
                pe.wait_ge(w_hi, w_base + c + 1)
                for j in range(2):
                    k = 2 * c + j
                    s, s2 = k % 4, k % 2
                    pe.wait_ge(hi_done, base + k + 1)
                    if first and j:
                        pe.wait_ge(gated, T // 4 + 2)
                    for part, sm_ in ((Whi, w_hi), (Wlo, w_lo)):
                        if part is Wlo:
                            pe.wait_ge(w_lo, w_base + c + 1)
                        for b in range(2):
                            for n in range(2):
                                mm(bank(b * 4 + j * 2 + n), part[c % 2][:, b * P:(b + 1) * P],
                                   whi[:, s * HALF + n * 512:s * HALF + (n + 1) * 512],
                                   start=first and part is Whi, stop=False, skip_group_check=True)
                    pe.wait_ge(lo_done, base + k + 1)
                    for b in range(2):
                        for n in range(2):
                            last = mm(bank(b * 4 + j * 2 + n), Whi[c % 2][:, b * P:(b + 1) * P],
                                      wlo[:, s2 * HALF + n * 512:s2 * HALF + (n + 1) * 512],
                                      start=False, stop=True, skip_group_check=True)
                    last.then_inc(half_done, 1)

            pe.wait_ge(bank_free, 2 + F_V)
            value_block(2 * F_V, 0, 0, True)
            value_block(2 * F_V, 1, 0, False)
            with pe.Fori(0, B_V // 2 - 1) as i:
                for q in range(2):
                    value_block(i * 4 + 2 * F_V + 4, q, i * 2 + 2, False)

        @block.scalar
        def _(act):
            A = nc.scalar.activation
            ch = Chain(act, act_s)
            eps = C["eps"]

            for k in range(0, KC, 4):
                act.wait_ge(x_loaded[k // 4], 16)
                A(hn[:, k:k + 4, :], xT[:, k:k + 4, :], ACT.Square).then_inc(sq_done, 1)
            hi_half(act, 0, 0)
            act.wait_ge(first_loaded, 16)
            A(scal[:, 8:9], C["eps"], ACT.Sqrt)
            act.wait_ge(ms_done, 1)
            A(rstd0, bank(7, 0, L), ACT.Sqrt, bias=eps).then_inc(std_done, 1)
            act.wait_ge(params_loaded, 16)
            A(wf_hi, C["w_forget"], ACT.Copy).then_inc(wf_split, 1)
            hi_half(act, 0, 1)
            act.nop().then_inc(bank_free, 2)
            act.nop().then_inc(o_ready, 1)
            for a, b in PIECES:
                act.wait_ge(normed, b)
                A(xhi[:, a:b, :], hn[:, a:b, :], ACT.Copy).then_inc(split_hi, 1)
            hi_half(act, 0, 2)
            z8 = fg[0][0:HEADS, :]
            act.wait_ge(forget_ps, 1)
            hi_half(act, 0, 3)
            A(z8, psum[0:HEADS, 6 * 512:6 * 512 + L], ACT.Identity, bias=C["b_forget"][0:HEADS, :]).then_inc(forget_z, 1)
            act.wait_ge(lam_dots, 1)
            A(scal[:, 4:6], scal[:, 2:4], ACT.Exp).then_inc(lam_exp, 1)
            act.wait_ge(forget_abs, 1)
            ch.link(A(fg[2][0:HEADS, :], fg[1][0:HEADS, :], ACT.Exp))
            A(fg[3][0:HEADS, :], fg[2][0:HEADS, :], ACT.Ln, bias=C["one"][0:HEADS, 0:1]).then_inc(forget_e, 1)

            with act.Fori(0, HEADS) as i:
                names = ["dq", "dk", "fq", "fk"]
                for p in range(PER_HEAD):
                    if p == 9:
                        act.wait_ge(half_done, i * 20 + 2 * p + 1)
                        hi_half(act, i * 20, 2 * p + 4)
                        A(sm[:, 18:19], C["eps"], ACT.Sqrt)
                    act.wait_ge(half_done, i * 20 + 2 * p + 2)
                    if p < 4:
                        at, n = QK_AT[names[p]]
                        A(qk_raw[:, at:at + n], bank(p % 2, 0, n), ACT.Copy)
                        A(qk_sq[:, at:at + n], bank(p % 2, 0, n), ACT.Square).then_inc(bank_free, 1)
                    elif p < 6:
                        A(vT[p - 4], bank(p % 2, 0, L), ACT.Copy).then_inc(bank_free, 1)
                    else:
                        g = i * 4 + (p - 6)
                        A(gates[:, ds(g, 1), :].rearrange("p a t -> p (a t)"), bank(p % 2, 0, T), ACT.Identity,
                          bias=C["b_gate"][:, ds(g, 1)]).then_inc(bank_free, 1)
                    if p == 9:
                        act.wait_ge(o_ms, i + 1)
                        A(o_std, bank(7, 0, T), ACT.Sqrt, bias=eps).then_inc(o_std_done, 1)
                    for j in range(2):
                        if (p, j) != (9, 0):
                            hi_half(act, i * 20, 2 * p + 4 + j)
                    if p == 3:
                        act.wait_ge(cum_moved, 32 * HEADS)
                        first, second, minus = (C["rows01"][0:2, n:n + 1] for n in range(3))
                        A(cum_q[0:2, :], cum_rows[0:2, ds(i * L + META, T)], ACT.Identity, scale=first, bias=second)
                        A(cum_k[0:2, :], cum_rows[0:2, ds(i * L, L)], ACT.Identity, scale=minus,
                          bias=first).then_inc(cum_fixed, 1)
                    if p in (2, 4):
                        q, k = (("dq", "dk"), ("fq", "fk"))[p // 2 - 1]
                        act.wait_ge(head_ms, i * 2 + p // 2)
                        at, n = QK_AT[q]
                        A(qk_std[:, at:at + n], bank(2, 0 if p == 2 else T, T), ACT.Sqrt, bias=eps)
                        at, n = QK_AT[k]
                        A(qk_std[:, at:at + n], bank(3 if p == 2 else 4, 0, L), ACT.Sqrt,
                          bias=eps).then_inc(head_std, 1)
                    if p in (5, 6):
                        j, b = p - 5, (7, 5)[p - 5]
                        act.wait_ge(vt_done, i * 2 + j + 1)
                        A(v[j][0:META, 0:P], psum[0:META, b * 512:b * 512 + P], ACT.Copy)
                        A(v[j][:, P:3 * P], bank(b, P, 2 * P), ACT.Copy).then_inc(v_ready, 1)
                        for c in ((0, 1), (2,))[j]:
                            act.wait_ge(masked, i * 3 + c + 1)
                            for n, keys in enumerate(KEYS):
                                s = prob[c][:, n * KEYS[0]:n * KEYS[0] + keys]
                                last = A(s, s, ACT.Exp, scale=-1.0, bias=neg_max[:, 2 * c + n:2 * c + n + 1],
                                         accum_out=zsum[:, 2 * c + n:2 * c + n + 1])
                            last.then_inc(exped, 1)
                    if p in (8, 9):
                        j = p - 8
                        act.wait_ge(pv_done, i * 2 + j + 1)
                        if j == 0:
                            A(o_sq, bank(2, 0, T), ACT.Square)
                        A(oT[:, ds(i, 1), j, :].rearrange("p a t -> p (a t)"), bank(2, j * T, T),
                          ACT.Copy).then_inc(o_ready, 1)

            act.wait_ge(o_ready, 2 * HEADS + 1)
            for a, b in PIECES:
                if a == HEADS:
                    act.wait_ge(heads_normed, HEADS)
                A(yhi[:, a:b, :], oT[:, a % HEADS:a % HEADS + b - a, 0 if a >= HEADS else 1, :],
                  ACT.Copy).then_inc(split_hi, 1)
            def sigmoids(i, q):
                gs = [gates[:, ds(i * 2 + q + KC * n, 1), :].rearrange("p a t -> p (a t)") for n in range(2)]
                A(gs[0], gs[0], ACT.Sigmoid)
                A(gs[1], gs[1], ACT.Sigmoid).then_inc(sig_done, 1)

            def branch_hi(i, m):
                act.wait_ge(half_done, i * 4 + (2 * F_BRANCH + m + 1))
                hi_half(act, i * 4 + 2 * F_BRANCH, m + 4)

            last = B_BRANCH // 2 - 1
            with act.Fori(0, last) as i:
                for q in range(2):
                    sigmoids(i, q)
                    branch_hi(i, 2 * q)
                    branch_hi(i, 2 * q + 1)
            for q in range(2):
                sigmoids(last, q)
            for m in range(3):
                branch_hi(last, m)
            for a, b in PIECES:
                if a == HEADS:
                    act.wait_ge(half_done, 2 * F_OUT)
                act.wait_ge(bank_free, 2 + F_BRANCH + b)
                A(yhi[:, a:b, :], merged[:, a:b, :], ACT.Copy).then_inc(split_hi, 1)
            branch_hi(last, 3)
            with act.Fori(0, B_OUT // 2) as i:
                for q in range(2):
                    for j in range(2):
                        act.wait_ge(half_done, i * 4 + (2 * F_OUT + 2 * q + j + 1))
                        if j:
                            act.wait_ge(bank_free, i * 2 + (F_OUT + q + 3))
                            A(h2_sq[:, ds(i * 2 + q, 1), :], h1T[:, ds(i * 2 + q, 1), :], ACT.Square
                              ).then_inc(sq_done, 1)
                        hi_half(act, i * 4 + 2 * F_OUT, 2 * q + 4 + j)
            A(scal[:, 8:9], C["one"][:, 0:1], ACT.Sqrt)
            act.wait_ge(ms_done, 2)
            A(rstd2, bank(7, 0, T), ACT.Sqrt, bias=eps).then_inc(std_done, 1)
            act.wait_ge(rows_ps, 1)
            A(rows[:, D + HALF:2 * D], bank(0, 0, HALF), ACT.Copy).then_inc(rows_act, 1)
            for a, b in PIECES:
                act.wait_ge(normed, KC + b)
                A(yhi[:, a:b, :], h2[:, a:b, :], ACT.Copy).then_inc(split_hi, 1)
            act.wait_ge(rows_ps, 3)
            A(rows[:, 0:D], bank(2, 0, D), ACT.Copy)
            A(rows[:, D:D + HALF], bank(6, 0, HALF), ACT.Copy).then_inc(rows_act, 1)
            act.wait_ge(rows_act, 2)
            act.dma_start(h1_rows, rows).then_inc(rows_out, 16)

            def query(i, q):
                act.wait_ge(half_done, i * 4 + (2 * F_QUERY + 2 * q + 2))
                A(qT[:, ds(i * 2 + q, 1), :].rearrange("p a t -> p (a t)"), bank(q, 0, T),
                  ACT.Copy).then_inc(bank_free, 1)

            with act.Fori(0, B_QUERY // 2) as i:
                for q in range(2):
                    query(i, q)
                    for j in range(2):
                        hi_half(act, i * 4 + 2 * F_QUERY, 2 * q + 4 + j)
            act.wait_ge(key_scores, 1)
            for c in range(2):
                last = A(st[:, 0:HEADS, c, :], bank(SCORES[0][c], 0, HEADS * NK).rearrange("p (h n) -> p h n", h=HEADS),
                         ACT.Copy)
            last.then_inc(scores_sb, 1)
            def one_weight(chunk):
                return W[:, ds(chunk, 1), :].rearrange("p a t -> p (a t)")

            act.wait_ge(scores_sb, 1)
            act.wait_ge(scores_dve, 1)
            with act.Fori(0, 2 * HEADS) as i:
                act.wait_ge(sc_taken, i + 1)
                A(sc, st[:, ds(i, 1), :, :].rearrange("p a c n -> p (a c) n"), ACT.Copy).then_inc(sc_ready, 1)
                for q in range(4):
                    act.wait_ge(half_done, i * 8 + (2 * F_U + 2 * q + 2))
                    A(one_weight(i * 4 + q), bank(q % 2, 0, T), ACT.Gelu).then_inc(bank_free, 1)
                    for j in range(2):
                        hi_half(act, i * 8 + 2 * F_U, 2 * q + 4 + j)
            A(gate_sum[:, 0:1], C["eps"], ACT.Exp)
            act.wait_ge(best_sub, 1)
            A(chosen_g, chosen_g, ACT.Exp).then_inc(best_exp, 1)
            act.wait_ge(gate_split, 1)

            def scale_rows(i, u):
                act.wait_ge(row_ready, i * 4 + (u + 1))
                for t in range(2):
                    for n in range(2):
                        last = A(hots[:, u % 2, t, 1 + n, :], row2[:, u % 2, t, :], ACT.Copy,
                                 scale=f(gate_sb[n][:, ds(i * 8 + (2 * u + t), 1)]))
                last.then_inc(hot, 1)

            def act_late_slot(i, m):
                act.wait_ge(half_done, i * 4 + (2 * F_G + m + 1))
                if m % 2:
                    A(bank(m // 2 % 2, 0, T), bank(m // 2 % 2, 0, T), ACT.Gelu).then_inc(gelu_done, 1)
                hi_half(act, i * 4 + 2 * F_G, m + 4)

            scale_rows(0, 0)
            act_late_slot(0, 0)
            scale_rows(0, 1)
            with act.Fori(0, B_U // 4 - 1) as i:
                for m in range(1, 5):
                    act_late_slot(i, m)
                    scale_rows(i, m + 1)
            for m in range(B_U - 3, B_U):
                act_late_slot(0, m)
                if m < B_U - 1:
                    scale_rows(0, m + 1)

            def weight_hi(chunk, q):
                A(Whi[q], one_weight(chunk), ACT.Copy).then_inc(w_hi, 1)

            act.wait_ge(half_done, 2 * F_V)
            act.wait_ge(first_weights, 1)
            act.wait_ge(bank_free, 2 + F_V)
            for q in range(2):
                weight_hi(q, q)
            with act.Fori(0, B_V // 2 - 1) as i:
                for q in range(2):
                    act.wait_ge(half_done, i * 4 + (2 * F_V + 2 * q + 2))
                    act.wait_ge(gated, T // 4 + 2)
                    weight_hi(i * 2 + (2 + q), q)
                    for j in range(2):
                        hi_half(act, i * 4 + 2 * F_V, 2 * q + 4 + j)

        @block.gpsimd
        def _(pool):
            pool.wait_ge(cum_done, 1)
            for h in range(HEADS):
                for r in range(2):
                    pool.dma_start(cum_rows[r:r + 1, h * L:(h + 1) * L], fg[2][h:h + 1, :]).then_inc(cum_moved, 16)
            a = r_work.a
            pool.wait_ge(rows_ps, 3)
            pool.wait_ge(key_scores, 2)
            nc.gpsimd.memset(arena[:, a + SPARE // 2:a + SPARE], 1.0)
            pool.wait_ge(rows_out, 16)
            nc.gpsimd.memset(arena[:, r_o.a:r_o.b], 1.0).then_inc(ones_early, 1)
            pool.wait_ge(choice_ps, 1)
            pool.wait_ge(const_used, 1)
            nc.gpsimd.memset(arena[:, a:a + SPARE // 2], 1.0)
            nc.gpsimd.memset(arena[:, a + SPARE:r_o.a], 1.0)
            nc.gpsimd.memset(arena[:, r_o.b:NK * T], 1.0).then_inc(ones_late, 1)

        @block.vector
        def _(dve):
            V = nc.vector
            ch = Chain(dve, dve_s)

            for n in range(4):
                dve.wait_ge(sq_done, n + 1)
                V.tensor_reduce(sums[n], hn[:, 4 * n:4 * n + 4, :].rearrange("p k t -> p t k"), AX.X,
                                ALU.add).then_inc(sums_done, 1)
            lo_half(dve, 0, 0)
            dve.wait_ge(std_done, 1)
            ch.link(V.reciprocal(rstd0, rstd0))

            def x_lo(n):
                a, b = PIECES[n]
                dve.wait_ge(split_hi, n + 1)
                V.tensor_tensor(xlo[:, a:b, :], hn[:, a:b, :], f(xhi[:, a:b, :]), ALU.subtract).then_inc(split_lo, 1)

            dve.wait_ge(params_loaded, 16)
            for n, (a, b) in enumerate(PIECES):
                for k in range(a, b):
                    V.scalar_tensor_tensor(hn[:, k, :], xT[:, k, :], C["g_mix"][:, k:k + 1], rstd0, ALU.mult,
                                           ALU.mult).then_inc(normed, 1)
                if n:
                    x_lo(n - 1)
                else:
                    dve.wait_ge(wf_split, 1)
                    V.tensor_tensor(wf_lo, C["w_forget"], f(wf_hi), ALU.subtract).then_inc(wf_rest, 1)
            x_lo(len(PIECES) - 1)
            lo_half(dve, 0, 1)
            for n in range(2):
                a = C["lambdas"][:, n * 128:n * 128 + 64]
                b = C["lambdas"][:, n * 128 + 64:n * 128 + 128]
                last = V.tensor_tensor_reduce(out=lam_t, in0=a, in1=b, scale=1.0, scalar=0.0, op0=ALU.mult,
                                              op1=ALU.add, accum_out=scal[:, 2 + n:3 + n])
                if n == 0:
                    ch.link(last)
            last.then_inc(lam_dots, 1)
            ch.link(V.tensor_scalar(C["g_dq"], C["g_dq"], 64 ** -0.5, None, ALU.mult))
            ch.link(V.tensor_scalar(C["g_fq"], C["g_fq"], 128 ** -0.5, None, ALU.mult))
            ch.link(V.tensor_scalar(C["g_sub"], C["g_sub"], 1.0 - LAM_INIT, None, ALU.mult))
            dve.wait_ge(loaded, 16)
            dve.wait_ge(lam_exp, 1)
            ch.link(V.tensor_tensor(scal[:, 6:7], scal[:, 4:5], scal[:, 5:6], ALU.subtract))
            ch.link(V.tensor_scalar(neg_lam, scal[:, 6:7], -1.0, -LAM_INIT, ALU.mult, ALU.add))
            z, a_, e_, l_ = (fg[n][0:HEADS, :] for n in range(4))
            dve.wait_ge(forget_z, 1)
            ch.link(V.tensor_scalar(a_, z, -1.0, None, ALU.mult))
            V.tensor_tensor(a_, a_, z, ALU.min).then_inc(forget_abs, 1)
            dve.wait_ge(forget_e, 1)
            ch.link(V.tensor_scalar(z, z, 0.0, None, ALU.min))
            ch.link(V.tensor_tensor(z, z, l_, ALU.subtract))
            V.tensor_tensor_scan(e_, C["one"][0:HEADS, :].broadcast_to([HEADS, L]), z, 0.0, ALU.mult, ALU.add).then_inc(cum_done, 1)

            with dve.Fori(0, HEADS) as i:
                ch.enter(i, 10)

                def normed_piece(name):
                    at, n = QK_AT[name]
                    return V.scalar_tensor_tensor(qk[:, at:at + n], qk_raw[:, at:at + n], C["g_" + name],
                                                  qk_std[:, at:at + n], ALU.mult, ALU.mult)

                def mask_max(c, b):
                    for n, keys in enumerate(KEYS):
                        a = n * KEYS[0]
                        last = V.tensor_tensor_reduce(out=prob[c][:, a:a + keys], in0=bank(b, a, keys),
                                                      in1=C["mask"][:, a:a + keys], scale=-1.0, scalar=3e38,
                                                      op0=ALU.add, op1=ALU.min,
                                                      accum_out=neg_max[:, 2 * c + n:2 * c + n + 1])
                    last.then_inc(masked, 1)

                for p in range(PER_HEAD):
                    for j in range(2):
                        dve.wait_ge(half_done, i * 20 + 2 * p + j + 1)
                        if (p, j) != (7, 0):
                            lo_half(dve, i * 20, 2 * p + j + 2)
                        if (p, j) == (3, 0):
                            dve.wait_ge(head_std, i * 2 + 1)
                            ch.link(V.reciprocal(qk_std[:, 0:T + L], qk_std[:, 0:T + L]))
                        if (p, j) == (3, 1):
                            normed_piece("dq")
                            normed_piece("dk").then_inc(head_normed, 1)
                        if (p, j) == (4, 1):
                            dve.wait_ge(head_normed, i * 2 + 1)
                            dve.wait_ge(rot_done, i + 1)
                            ch.link(V.tensor_tensor(rope_a, psum[:, 6 * 512 - T:6 * 512 + L], C["rope_sin"], ALU.mult))
                            ch.link(V.tensor_tensor(rope_b, qk[:, 0:T + L], C["rope_cos"], ALU.mult))
                            V.tensor_tensor(qk[:, 0:T + L], rope_b, rope_a, ALU.add).then_inc(roped, 1)
                        if (p, j) == (5, 0):
                            dve.wait_ge(head_std, i * 2 + 2)
                            ch.link(V.reciprocal(qk_std[:, T + L:QK_W], qk_std[:, T + L:QK_W]))
                        if (p, j) == (5, 1):
                            normed_piece("fq")
                            normed_piece("fk").then_inc(head_normed, 1)
                            dve.wait_ge(scored, 1)
                            dve.wait_ge(scored, i * 2 + 1)
                            mask_max(0, 3)
                        if (p, j) == (6, 0):
                            mask_max(1, 6)
                        if (p, j) == (6, 1):
                            dve.wait_ge(scored, 2)
                            dve.wait_ge(scored, i * 2 + 2)
                            mask_max(2, 4)
                        if (p, j) == (7, 0):
                            dve.wait_ge(exped, i * 3 + 2)
                            ch.link(V.reciprocal(zinv[:, 0:4], zsum[:, 0:4]))
                            ch.link(V.tensor_scalar(zinv[:, 2:4], zinv[:, 2:4], neg_lam, None, ALU.mult))
                            for n, keys in enumerate(KEYS):
                                s = slice(n * KEYS[0], n * KEYS[0] + keys)
                                ch.link(V.tensor_scalar(prob[1][:, s], prob[1][:, s], zinv[:, 2 + n:3 + n], None,
                                                        ALU.mult))
                                last = V.scalar_tensor_tensor(prob[0][:, s], prob[0][:, s], zinv[:, n:n + 1],
                                                              prob[1][:, s], ALU.mult, ALU.add)
                            last.then_inc(prob_ready, 1)
                            lo_half(dve, i * 20, 2 * p + j + 2)
                        if (p, j) == (7, 1):
                            dve.wait_ge(exped, i * 3 + 3)
                            ch.link(V.reciprocal(zinv[:, 4:6], zsum[:, 4:6]))
                            for n, keys in enumerate(KEYS):
                                s = slice(n * KEYS[0], n * KEYS[0] + keys)
                                last = V.tensor_scalar(prob[2][:, s], prob[2][:, s], zinv[:, 4 + n:5 + n], None, ALU.mult)
                            last.then_inc(prob_ready, 1)
                        if (p, j) == (9, 1):
                            dve.wait_ge(o_std_done, i + 1)
                            ch.link(V.reciprocal(o_std, o_std))
                            o = oT[:, ds(i, 1), 0, :].rearrange("p a t -> p (a t)")
                            V.scalar_tensor_tensor(o, o, C["g_sub"], o_std, ALU.mult, ALU.mult
                                                   ).then_inc(heads_normed, 1)
                        if (p, j) in ((7, 1), (8, 1)):
                            c = p - 7
                            dve.wait_ge(pt_done, i * 2 + c + 1)
                            b = (3, 4)[c]
                            V.tensor_copy(pT[c][0:META, 0:T], psum[0:META, b * 512:b * 512 + T])
                            V.tensor_copy(pT[c][:, T:2 * T], bank(b, T, T))
                            V.tensor_copy(pT[c][:, 2 * T:2 * T + P],
                                          bank(7, 384, P) if c == 0 else bank(6, 0, P)).then_inc(pt_ready, 1)
                ch.leave(HEADS)

            def piece_lo(src, n, count):
                a, b = PIECES[n]
                dve.wait_ge(split_hi, count + n + 1)
                V.tensor_tensor(ylo[:, a:b, :], src, f(yhi[:, a:b, :]), ALU.subtract).then_inc(split_lo, 1)

            dve.wait_ge(heads_normed, HEADS)
            for n, (a, b) in enumerate(PIECES):
                piece_lo(oT[:, a % HEADS:a % HEADS + b - a, 0 if a >= HEADS else 1, :], n, 5)
            def merge_product(i, q, j):
                dve.wait_ge(half_done, i * 4 + (2 * F_BRANCH + 2 * q + j + 1))
                if j == 0:
                    lo_half(dve, i * 4 + 2 * F_BRANCH, 2 * q + 2)
                    dve.wait_ge(sig_done, i * 2 + q + 1)
                    dve.wait_ge(bank_free, i * 2 + (F_BRANCH + q + 2))
                g = gates[:, ds(i * 2 + q + KC * (1 - j), 1), :].rearrange("p a t -> p (a t)")
                ch.link(V.tensor_tensor(br[j], bank(2 * (1 - j) + q, 0, T), g, ALU.mult))

            def merge_sum(i, q):
                V.tensor_tensor(merged[:, ds(i * 2 + q, 1), :].rearrange("p a t -> p (a t)"), br[0], br[1],
                                ALU.add).then_inc(bank_free, 1)

            last = B_BRANCH // 2 - 1
            with dve.Fori(0, last) as i:
                ch.enter(i, 4)
                for q in range(2):
                    merge_product(i, q, 0)
                    merge_product(i, q, 1)
                    merge_sum(i, q)
                    lo_half(dve, i * 4 + 2 * F_BRANCH, 2 * q + 3)
                ch.leave(last)
            merge_product(last, 0, 0)
            merge_product(last, 0, 1)
            merge_sum(last, 0)
            lo_half(dve, last * 4 + 2 * F_BRANCH, 3)
            merge_product(last, 1, 0)
            for n, (a, b) in enumerate(PIECES):
                if a == HEADS:
                    merge_product(last, 1, 1)
                    merge_sum(last, 1)
                    dve.wait_ge(bank_free, 2 + F_OUT)
                piece_lo(merged[:, a:b, :], n, 10)
            lo_half(dve, last * 4 + 2 * F_BRANCH, 5)
            with dve.Fori(0, B_OUT // 2) as i:
                for q in range(2):
                    for j in range(2):
                        dve.wait_ge(half_done, i * 4 + (2 * F_OUT + 2 * q + j + 1))
                        if j:
                            V.tensor_tensor(h1T[:, ds(i * 2 + q, 1), :].rearrange("p a t -> p (a t)"), bank(q, 0, T),
                                            xT[:, ds(i * 2 + q, 1), META:L].rearrange("p a t -> p (a t)"),
                                            ALU.add).then_inc(bank_free, 1)
                        lo_half(dve, i * 4 + 2 * F_OUT, 2 * q + j + 2)
            dve.wait_ge(bank_free, 2 + F_QUERY)
            dve.wait_ge(std_done, 2)
            ch.link(V.reciprocal(rstd2, rstd2))
            for n, (a, b) in enumerate(PIECES):
                for k in range(a, b):
                    V.scalar_tensor_tensor(h2[:, k, :], h1T[:, k, :], C["g_peer"][:, k:k + 1], rstd2, ALU.mult,
                                           ALU.mult).then_inc(normed, 1)
                if n:
                    piece_lo(h2[:, PIECES[n - 1][0]:a, :], n - 1, 15)
            piece_lo(h2[:, PIECES[-1][0]:KC, :], len(PIECES) - 1, 15)
            with dve.Fori(0, B_QUERY // 2) as i:
                for q in range(2):
                    for j in range(2):
                        dve.wait_ge(half_done, i * 4 + (2 * F_QUERY + 2 * q + j + 1))
                        lo_half(dve, i * 4 + 2 * F_QUERY, 2 * q + j + 2)
            dve.nop().then_inc(sc_taken, 1)
            dve.nop().then_inc(gated, 2)
            dve.wait_ge(key_scores, 2)
            for c in range(2):
                last = V.tensor_copy(st[:, HEADS:2 * HEADS, c, :],
                                     bank(SCORES[1][c], 0, HEADS * NK).rearrange("p (h n) -> p h n", h=HEADS))
            last.then_inc(scores_dve, 1)

            ch.spare = small[:, 1280:1280 + 16]
            with dve.Fori(0, 2 * HEADS) as i:
                ch.enter(i, 15)
                mine = ds(i * TOPK, TOPK)
                for m in range(8):
                    dve.wait_ge(half_done, i * 8 + (2 * F_U + m + 1))
                    if m < 7:
                        lo_half(dve, i * 8 + 2 * F_U, m + 2)
                    if m == 0:
                        dve.wait_ge(sc_ready, i + 1)
                        ch.stand(0)
                        V.max(vals[:, 0, 0:8], sc[:, 0, :])
                        ch.link(V.max(vals[:, 1, 0:8], sc[:, 1, :]), True)
                        V.max_index(idxu[:, 0, 0:8], vals[:, 0, 0:8], sc[:, 0, :])
                    if m == 1:
                        V.max_index(idxu[:, 1, 0:8], vals[:, 1, 0:8], sc[:, 1, :])
                        V.match_replace(sc_left[:, 0, :], vals[:, 0, 0:8], sc[:, 0, :], LOWEST)
                        ch.link(V.match_replace(sc_left[:, 1, :], vals[:, 1, 0:8], sc[:, 1, :], LOWEST), True)
                    if m == 2:
                        V.max(vals[:, 0, 8:16], sc_left[:, 0, :])
                        ch.link(V.max(vals[:, 1, 8:16], sc_left[:, 1, :]), True)
                        V.max_index(idxu[:, 0, 8:16], vals[:, 0, 8:16], sc_left[:, 0, :])
                    if m == 3:
                        V.max_index(idxu[:, 1, 8:16], vals[:, 1, 8:16], sc_left[:, 1, :]).then_inc(sc_taken, 1)
                        dve.wait_ge(sc_taken, i + 2)
                        V.tensor_copy(idxf, idxu)
                        ch.link(V.tensor_tensor(cand.rearrange("p (a b) -> p a b", a=TOPK),
                                                spread(vals[:, 0, :].unsqueeze(2), 2, TOPK),
                                                spread(vals[:, 1, :].unsqueeze(1), 1, TOPK), ALU.add), True)
                    if m == 4:
                        ch.link(V.max(best[:, 0:8], cand), True)
                        V.max_index(ju[:, 0:8], best[:, 0:8], cand)
                        ch.link(V.match_replace(cand_left, best[:, 0:8], cand, LOWEST), True)
                    if m == 5:
                        ch.link(V.max(best[:, 8:16], cand_left), True)
                        ch.link(V.max_index(ju[:, 8:16], best[:, 8:16], cand_left))
                        V.tensor_scalar(jh[:, 0, :], ju, 4, None, ALU.logical_shift_right)
                        ch.link(V.tensor_scalar(jh[:, 1, :], ju, TOPK - 1, None, ALU.bitwise_and))
                    if m == 6:
                        ch.link(V.tensor_copy(jf, jh))
                        ch.link(V.tensor_tensor(eq, spread(jf.unsqueeze(3), 3, TOPK),
                                                spread(spread(C["iota16"].unsqueeze(1).unsqueeze(1), 1, 2), 2, TOPK),
                                                ALU.is_equal))
                    if m == 7:
                        ch.link(V.tensor_tensor(eq, eq, spread(idxf.unsqueeze(2), 2, TOPK), ALU.mult))
                        ch.link(V.tensor_copy(best_all[:, mine], best))
                        for c in range(2):
                            ch.link(V.tensor_reduce(chosen_i[:, c, mine], eq[:, c, :, :], AX.X, ALU.add))
                        lo_half(dve, i * 8 + 2 * F_U, m + 2)
                ch.leave(2 * HEADS)
            best3 = best_all.rearrange("p (i k) -> p i k", k=TOPK)
            gate3 = chosen_g.rearrange("p (i k) -> p i k", k=TOPK)
            V.tensor_tensor(gate3, best3, spread(best3[:, :, 0:1], 2, TOPK), ALU.subtract).then_inc(best_sub, 1)
            dve.wait_ge(best_exp, 1)
            ch.link(V.tensor_reduce(gate_sum[:, 0:2 * HEADS], gate3, AX.X, ALU.add))
            ch.link(V.reciprocal(gate_sum[:, 2 * HEADS:4 * HEADS], gate_sum[:, 0:2 * HEADS]))
            V.tensor_tensor(gate3, gate3, spread(gate_sum[:, 2 * HEADS:4 * HEADS].unsqueeze(2), 2, TOPK),
                            ALU.mult).then_inc(chosen, 1)
            V.tensor_copy(iota_bf, C["iota"]).then_inc(const_used, 1)
            dve.wait_ge(choice_ps, 1)
            rest = idx_ps[2]
            for n in range(3):
                ch.link(V.tensor_copy(part[n], rest))
                if n < 2:
                    ch.link(V.tensor_tensor(left[n], rest, part[n], ALU.subtract))
                    rest = left[n]
                last = V.tensor_copy((gate_sb + [idx_ps[3]])[n], part[n])
                if n < 2:
                    ch.link(last)
            last.then_inc(gate_split, 1)
            dve.wait_ge(gate_split, 1)

            def make_rows(i, u):
                if u >= 2:
                    dve.wait_ge(gate_ps, i * 4 + (u - 1))
                for t in range(2):
                    i1, i2, gate = (idx_ps[n][:, ds(i * 8 + (2 * u + t), 1)] for n in (0, 1, 3))
                    V.tensor_scalar(hots[:, u % 2, t, 0, :], iota_bf, i1, None, ALU.is_equal)
                    V.tensor_scalar(row2[:, u % 2, t, :], iota_bf, i2, None, ALU.is_equal)
                    last = V.tensor_scalar(hots[:, u % 2, t, 3, :], iota_bf, i2, gate, ALU.is_equal, ALU.mult)
                last.then_inc(row_ready, 1)

            def late_slot(i, m):
                dve.wait_ge(half_done, i * 4 + (2 * F_G + m + 1))
                lo_half(dve, i * 4 + 2 * F_G, m + 2)
                if m < B_U - 1:
                    make_rows(i, m + 1)
                if m % 2 == 0 and m:
                    apply_gelu(i, m // 2 - 1)
                if m % 2 and m > 1:
                    apply_gates(i, (m - 3) // 2)

            def apply_gates(i, n):
                dve.wait_ge(gate_ps, i * 4 + (2 * n + 2))
                dve.wait_ge(bank_free, i * 2 + (2 + F_G + n + 1))
                w = W[:, :, ds(i * 8 + 4 * n, 4)].rearrange("p c t -> p t c")
                V.tensor_tensor(w, w, bank(2 + n % 2).rearrange("p (t c) -> p t c", t=4), ALU.mult).then_inc(gated, 1)

            def apply_gelu(i, c):
                dve.wait_ge(gelu_done, i * 2 + (c + 1))
                dve.wait_ge(gated, i * 2 + (c + 2))
                w = W[:, ds(i * 2 + (B_U // 2 + c), 1), :].rearrange("p a t -> p (a t)")
                V.tensor_tensor(w, w, bank(c % 2, 0, T), ALU.mult).then_inc(bank_free, 1)

            make_rows(0, 0)
            for m in range(4):
                if m == 2:
                    dve.wait_ge(ones_early, 1)
                    dve.wait_ge(ones_late, 1)
                late_slot(0, m)
            with dve.Fori(0, B_U // 4 - 2) as i:
                for m in range(4, 8):
                    late_slot(i, m)
            for m in range(B_U - 4, B_U):
                late_slot(0, m)
            apply_gelu(0, B_U // 2 - 1)
            dve.wait_ge(gate_ps, T // 2)
            dve.wait_ge(bank_free, 2 + F_V)
            g = bank(2 + (T // 4 - 1) % 2).rearrange("p (t c) -> p t c", t=4)
            for a, b, signal in ((0, 2, first_weights), (2, NK, gated)):
                w = W[:, a:b, T - 4:T].rearrange("p c t -> p t c")
                V.tensor_tensor(w, w, g[:, :, a:b], ALU.mult).then_inc(signal, 1)

            def weight_lo(chunk, q, n):
                dve.wait_ge(w_hi, n)
                V.tensor_tensor(Wlo[q], W[:, ds(chunk, 1), :].rearrange("p a t -> p (a t)"), f(Whi[q]),
                                ALU.subtract).then_inc(w_lo, 1)

            for q in range(2):
                weight_lo(q, q, q + 1)
            with dve.Fori(0, B_V // 2 - 1) as i:
                for q in range(2):
                    dve.wait_ge(half_done, i * 4 + (2 * F_V + 2 * q + 1))
                    lo_half(dve, i * 4 + 2 * F_V, 2 * q + 2)
                    dve.wait_ge(half_done, i * 4 + (2 * F_V + 2 * q + 2))
                    lo_half(dve, i * 4 + 2 * F_V, 2 * q + 3)
                    dve.wait_ge(gated, T // 4 + 2)
                    weight_lo(i * 2 + (2 + q), q, i * 2 + (3 + q))
            for j in range(2):
                dve.wait_ge(half_done, 2 * BLOCKS - 4 + j + 1)
                lo_half(dve, 2 * BLOCKS - 4, j + 2)
            for at, n in enumerate(OUT_ORDER):
                dve.wait_ge(half_done, 2 * BLOCKS - (1 if at < 4 else 0))
                dve.wait_ge(rows_back[n // 2], 16)
                V.tensor_tensor(arena[:, n * 512:(n + 1) * 512], bank(n), raw[:, n * 512:(n + 1) * 512],
                                ALU.add).then_inc(out_sb, 1)


def lay_out(inputs):
    w_in = inputs["w_in"][0]
    n = HEADS * P
    cuts = np.cumsum([0, n, n, n, n, n, n, HEADS, D, D])
    dq, dk, dv, fq, fk, fv, wf, ga, gb = (w_in[:, a:b] for a, b in zip(cuts[:-1], cuts[1:]))
    gate_cols = np.concatenate([ga, gb], 1)
    order = []
    for h in range(HEADS):
        s = slice(h * P, (h + 1) * P)
        order += [dq[:, s], dk[:, s], fq[:, s], fk[:, s], dv[:, s], fv[:, s], gate_cols[:, h * 4 * P:(h + 1) * 4 * P]]
    branch = np.concatenate([inputs["w_branch_fox"][0], inputs["w_branch_diff"][0]], 0)
    cols = np.concatenate(order + [branch, inputs["w_out"][0], inputs["peer_w_query"][0]], 1)
    first = cols.reshape(KC, P, F_U, P).transpose(2, 1, 0, 3).reshape(F_U, P, D)
    u = inputs["peer_expert_u"][0].reshape(P, NK, KC, P).transpose(1, 3, 2, 0).reshape(B_U, P, D)
    v = inputs["peer_expert_v"][0].reshape(P, NK, D).transpose(1, 0, 2)
    stream = np.empty((BLOCKS, 2, P, HALF), np.float32)
    for at, part in ((0, first), (F_U, u), (F_V, v)):
        stream[at:at + len(part)] = part.reshape(len(part), P, 2, HALF).transpose(0, 2, 1, 3)
    stream = stream.reshape(2 * BLOCKS, P, HALF)

    tokens = np.concatenate([inputs["meta_tokens"], inputs["x"][0]], 0)
    x_t = np.ascontiguousarray(tokens.T.reshape(KC, P, L).transpose(1, 0, 2).reshape(P, KC * L))

    at, width = columns(PARAMS)
    params = np.zeros((P, width), np.float32)

    def put(name, v):
        a, w = at[name]
        params[0:v.shape[0], a:a + w] = v

    put("g_mix", inputs["norm_mix_g"][0].reshape(KC, P).T)
    put("g_peer", inputs["norm_peer_g"][0].reshape(KC, P).T)
    put("b_gate", inputs["b_gate"][0].reshape(2 * KC, P).T)
    put("g_dq", np.tile(inputs["diff_q_norm_g"][0], 2)[:, None])
    put("g_dk", np.tile(inputs["diff_k_norm_g"][0], 2)[:, None])
    put("g_fq", inputs["fox_q_norm_g"][0][:, None])
    put("g_fk", inputs["fox_k_norm_g"][0][:, None])
    put("g_sub", inputs["diff_subln_g"][0][:, None])
    put("b_forget", inputs["b_forget"][0][:, None])
    lam = np.concatenate([inputs[n][0] for n in ("lambda_q1", "lambda_k1", "lambda_q2", "lambda_k2")])
    put("lambdas", np.broadcast_to(lam, (P, 256)))
    put("w_forget", wf.reshape(KC, P, HEADS).transpose(1, 0, 2).reshape(P, KC * HEADS))
    put("sub_keys", inputs["peer_sub_keys"][0].transpose(1, 3, 0, 2).reshape(P, HEADS * NK))
    return {"stream": stream, "x_t": x_t, "params": params, "consts": shape_constants()}


def kernel(**inputs):
    import concourse.bacc as bacc
    from concourse.bass_utils import run_bass_kernel_spmd

    inputs = {k: np.asarray(v) for k, v in inputs.items()}
    arrays = lay_out(inputs)
    nc = bacc.Bacc("TRN2", target_bir_lowering=False, num_devices=1)
    aps = {n: nc.dram_tensor(n, a.shape, F32, kind="ExternalInput").ap() for n, a in arrays.items()}
    h1_rows = nc.dram_tensor("h1_rows", (P, 2 * D), F32, kind="Internal").ap()
    out = nc.dram_tensor("out", (T, D), F32, kind="ExternalOutput").ap()
    hybrid_layer(nc, aps["stream"], aps["x_t"], aps["params"], aps["consts"], h1_rows, out)
    r = run_bass_kernel_spmd(nc, [arrays], core_ids=[0])
    return r.results[0]["out"].reshape(1, T, D)
```
